# Optimizing a Trainium2 kernel written in Bass

```python
import jax, jax.numpy as jnp
from jax import lax
import numpy as np

D_MODEL = 1024
BATCH = 1
SEQ = 512
DEPTH = 2

EXPAND = 2
E_WIDTH = EXPAND * D_MODEL
CONV_W = 3
CHUNK = 128
SG_HEADS = 8
SG_HEAD_DIM = E_WIDTH // SG_HEADS
N_MIXERS = 2
N_A = (DEPTH + 1) // 2
N_B = DEPTH // 2
EPS = 1e-6

kernel_name = "hybrid_shortconv_gmlp_adaln_encoder"

def _rmsnorm(x, g):
    xf = x.astype(jnp.float32)
    y = xf * lax.rsqrt(jnp.mean(xf * xf, axis=-1, keepdims=True) + EPS)
    return (y * g.astype(jnp.float32)).astype(x.dtype)

def _layernorm(x, g, b):
    xf = x.astype(jnp.float32)
    mu = jnp.mean(xf, axis=-1, keepdims=True)
    var = jnp.mean(jnp.square(xf - mu), axis=-1, keepdims=True)
    y = (xf - mu) * lax.rsqrt(var + EPS)
    return (y * g.astype(jnp.float32) + b.astype(jnp.float32)).astype(x.dtype)

def _modulation(c, w_mod, b_mod):
    m = jax.nn.silu(c) @ w_mod + b_mod
    shift, scale, gate = jnp.split(m, 3, axis=-1)
    return shift[:, None, :], scale[:, None, :], gate[:, None, :]

def _short_conv_mixer(h, w_in, w_conv, w_out):
    proj = h @ w_in
    z, bg, cg, xh = jnp.split(proj, 4, axis=-1)
    y = cg * xh
    yp = jnp.pad(y, ((0, 0), (1, 1), (0, 0)))
    y = (yp[:, :-2] * w_conv[:, 0] + yp[:, 1:-1] * w_conv[:, 1]
         + yp[:, 2:] * w_conv[:, 2])
    y = bg * y * jax.nn.silu(z)
    return y @ w_out

def _spatial_gating_mixer(h, w_in, ln_g, ln_b, w_s, b_s, w_out):
    bsz, s, _ = h.shape
    proj = h @ w_in
    z = proj[..., :E_WIDTH]
    uv = jax.nn.gelu(proj[..., E_WIDTH:], approximate=False)
    u, v = jnp.split(uv, 2, axis=-1)
    v = _layernorm(v, ln_g, ln_b)
    vc = v.reshape(bsz, s // CHUNK, CHUNK, SG_HEADS, SG_HEAD_DIM)
    sv = jnp.einsum('gpq,bnqge->bnpge', w_s, vc) + b_s.T[None, None, :, :, None]
    sv = sv.reshape(bsz, s, E_WIDTH)
    y = u * sv * jax.nn.silu(z)
    return y @ w_out

def setup_inputs(seed: int = 0) -> dict:
    key = jax.random.key(seed)
    ks = jax.random.split(key, 16)
    f32 = jnp.float32
    D, E = D_MODEL, E_WIDTH
    x = jax.random.normal(ks[0], (BATCH, SEQ, D), f32)
    c = jax.random.normal(ks[1], (BATCH, D), f32)
    norm_g = 1.0 + 0.05 * jax.random.normal(ks[2], (DEPTH, D), f32)
    w_mod = 0.2 * D ** -0.5 * jax.random.normal(ks[3], (DEPTH, D, 3 * D), f32)
    b_mod = 0.02 * jax.random.normal(ks[4], (DEPTH, 3 * D), f32)
    a_w_in = D ** -0.5 * jax.random.normal(ks[5], (N_A, D, 4 * E), f32)
    a_w_conv = CONV_W ** -0.5 * jax.random.normal(ks[6], (N_A, E, CONV_W), f32)
    a_w_out = E ** -0.5 * jax.random.normal(ks[7], (N_A, E, D), f32)
    b_w_in = D ** -0.5 * jax.random.normal(ks[8], (N_B, D, 3 * E), f32)
    b_ln_g = 1.0 + 0.05 * jax.random.normal(ks[9], (N_B, E), f32)
    b_ln_b = 0.02 * jax.random.normal(ks[10], (N_B, E), f32)
    b_w_s = CHUNK ** -0.5 * jax.random.normal(ks[11], (N_B, SG_HEADS, CHUNK, CHUNK), f32)
    b_b_s = 1.0 + 0.1 * jax.random.normal(ks[12], (N_B, SG_HEADS, CHUNK), f32)
    b_w_out = E ** -0.5 * jax.random.normal(ks[13], (N_B, E, D), f32)
    final_g = 1.0 + 0.05 * jax.random.normal(ks[14], (D,), f32)
    return {"x": x, "c": c, "norm_g": norm_g, "w_mod": w_mod, "b_mod": b_mod,
            "a_w_in": a_w_in, "a_w_conv": a_w_conv, "a_w_out": a_w_out,
            "b_w_in": b_w_in, "b_ln_g": b_ln_g, "b_ln_b": b_ln_b,
            "b_w_s": b_w_s, "b_b_s": b_b_s, "b_w_out": b_w_out,
            "final_g": final_g}

def reference(x, c, norm_g, w_mod, b_mod, a_w_in, a_w_conv, a_w_out,
              b_w_in, b_ln_g, b_ln_b, b_w_s, b_b_s, b_w_out, final_g):
    for i in range(DEPTH):
        shift, scale, gate = _modulation(c, w_mod[i], b_mod[i])
        h = _rmsnorm(x, norm_g[i]) * (1.0 + scale) + shift
        j = i // N_MIXERS
        if i % N_MIXERS == 0:
            y = _short_conv_mixer(h, a_w_in[j], a_w_conv[j], a_w_out[j])
        else:
            y = _spatial_gating_mixer(h, b_w_in[j], b_ln_g[j], b_ln_b[j],
                                      b_w_s[j], b_b_s[j], b_w_out[j])
        x = x + gate * y
    return _rmsnorm(x, final_g)


_drawn_inputs = setup_inputs


def setup_inputs(seed=0):
    import zlib

    import numpy as np

    out = dict(_drawn_inputs(seed))
    spreads = {}
    factors = {'norm_g': 5.288, 'b_mod': 3.064, 'b_ln_g': 45.952, 'b_ln_b': 189.746, 'b_b_s': 23.921}
    for name, (base, spread) in spreads.items():
        noise = np.random.default_rng([zlib.crc32(name.encode()), seed]).standard_normal(out[name].shape)
        drawn = base * np.exp(spread * noise) if base else spread * noise
        out[name] = __import__('jax').numpy.asarray(drawn.astype(out[name].dtype))
    for name, factor in factors.items():
        out[name] = (out[name] * factor).astype(out[name].dtype)
    return out
```

```python
from contextlib import ExitStack

import numpy as np

import concourse.bass as bass
from concourse import mybir

F32 = mybir.dt.float32
F32R = mybir.dt.float32r
ACT = mybir.ActivationFunctionType
ALU = mybir.AluOpType

P = 128
D = 1024
S = 512
E = 2048
KD = D // P
KE = E // P
NCH = S // P
EPS = 1e-6

SLOT = 1024
RING = 4
FREE = 2
LEAD = 3
PAIRS = KE // 2
DPAIRS = KD // 2

MOD_START = 16
W_AOUT = 8 * PAIRS
W_BV = W_AOUT + 4 * DPAIRS
W_BUZ = W_BV + 16
W_BOUT = W_BUZ + 4 * PAIRS
W_END = W_BOUT + 4 * DPAIRS
Q_END = MOD_START + 4 * PAIRS + W_END
Q_MINUS_W = Q_END - W_END
A_ORDER = ["m0", 0, 1, "m1", 2, 3, "m2", 4, "m3", 5, 6, 7]
A_MOD_AT = [A_ORDER.index(f"m{k}") for k in range(4)]
A_W_AT = [A_ORDER.index(k) for k in range(8)]
A_Q0 = MOD_START + LEAD

C_NORM = 0
C_BMOD = C_NORM + 2 * KD
C_C = C_BMOD + 6 * KD
C_LNG = C_C + KD
C_LNB = C_LNG + KE
C_FG = C_LNB + KE
C_CONV = C_FG + KD
N_COL = C_CONV + 3 * KE


def build(nc, stream, xt, cols_d, wst_d, bs_d, out):
    ctx = ExitStack()
    with ctx:
        def sb(name, shape, dt=F32):
            return ctx.enter_context(nc.sbuf_tensor(name, shape, dt))

        def sem(name):
            return ctx.enter_context(nc.semaphore(name))

        raw = sb("raw", [P, RING, SLOT])
        w_hi = sb("w_hi", [P, RING, SLOT], F32R)
        w_lo = sb("w_lo", [P, RING, SLOT], F32R)
        x = sb("x", [P, KD, S])
        h_hi = sb("h_hi", [P, KD, S], F32R)
        h_lo = sb("h_lo", [P, KD, S], F32R)
        y_hi = sb("y_hi", [P, KE, S], F32R)
        y_lo = sb("y_lo", [P, KE, S], F32R)
        ws_hi = sb("ws_hi", [P, 8 * P], F32R)
        ws_lo = sb("ws_lo", [P, 8 * P], F32R)
        vn_hi = sb("vn_hi", [P, 2, S], F32R)
        vn_lo = sb("vn_lo", [P, 2, S], F32R)
        rs_bc = sb("rs_bc", [P, 8 * P])
        bs_bc = sb("bs_bc", [P, 8 * P])
        tmp = sb("tmp", [P, 4, S])
        work = sb("work", [P, 2, S])
        ssum = sb("ssum", [P, S])
        term = sb("term", [P, 2, P])
        acc = sb("acc", [P, 2, 256])
        cols = sb("cols", [P, N_COL])
        silu_c = sb("silu_c", [P, KD])
        mod = sb("mod", [P, 6 * KD])
        amp = sb("amp", [P, 2 * KD])
        small = sb("small", [P, 8, 4])
        bstat = sb("bstat", [P, NCH, 4, 6])
        mv = sb("mv", [P, NCH, 2])
        ident = sb("ident", [P, P])
        ones = sb("ones", [P, P])
        ones_r = sb("ones_r", [P, P], F32R)

        pp = [ctx.enter_context(nc.psum_tensor(f"pp{b}", [P, S], F32)) for b in range(4)]
        p_small = ctx.enter_context(nc.psum_tensor("p_small", [P, S], F32))
        p_rstd = ctx.enter_context(nc.psum_tensor("p_rstd", [P, S], F32))
        p_sv = [ctx.enter_context(nc.psum_tensor(f"p_sv{u}", [P, S], F32)) for u in range(2)]

        landed = [sem(f"landed{j}") for j in range(RING)]
        consumed = sem("consumed")
        hi_cut = sem("hi_cut")
        blocks = sem("blocks")
        cols_in, x_in, ws_in, bs_in = sem("cols_in"), [sem(f"x_in{k}") for k in range(4)], sem("ws_in"), sem("bs_in")
        consts = sem("consts")
        sc_ready = sem("sc_ready")
        acc_used = sem("acc_used")
        ws_hi_cut, ws_cut = sem("ws_hi_cut"), sem("ws_cut")
        rs_summed = sem("rs_summed")
        sq_ready = sem("sq_ready")
        sq_added = sem("sq_added")
        stat_sum, var_ready, sd_ready = sem("stat_sum"), sem("var_ready"), sem("sd_ready")
        diag_ready, rstd_bc = sem("diag_ready"), sem("rstd_bc")
        h_made, h_hi_cut, h_cut = sem("h_made"), sem("h_hi_cut"), sem("h_cut")
        cg_ready, xh_used, sz_ready, bg_used = sem("cg_ready"), sem("xh_used"), sem("sz_ready"), sem("bg_used")
        y_cut = sem("y_cut")
        x_updated = sem("x_updated")
        v_gelu, v_cut = sem("v_gelu"), sem("v_cut")
        u_gelu = sem("u_gelu")
        vn_cut, sv_done, sv_used = sem("vn_cut"), sem("sv_done"), sem("sv_used")
        z_silu = sem("z_silu")
        out_ready, out_sent = sem("out_ready"), sem("out_sent")
        dve_step = sem("dve_step")

        def q_round(q):
            return 16 * (q // RING + 1)

        free_at_start = {"act": [sz_ready, u_gelu, z_silu], "pe": [sv_done], "dve": [bg_used, y_cut, x_updated, v_cut]}

        block = ctx.enter_context(nc.Block())

        @block.sync
        def _(sp):
            for q in range(RING):
                sp.dma_start(raw[:, q, :], stream[q, :, :]).then_inc(landed[q], 16)
            with sp.Fori(1, Q_END // RING) as r:
                for j in range(RING):
                    sp.wait_ge(consumed, RING * r + (j - RING + 1))
                    sp.dma_start(raw[:, j, :], stream[RING * r + j, :, :]).then_inc(landed[j], 16)
            for k in range(KD):
                sp.wait_ge(out_ready, k + 1)
                sp.dma_start(out[k, :, :], x[:, k, :]).then_inc(out_sent, 16)
            sp.wait_ge(out_sent, 16 * KD)

        @block.gpsimd
        def _(pool):
            pool.memset(ident[:, :], 0.0).then_inc(consts, 1)
            pool.memset(ones[:, :], 1.0).then_inc(consts, 1)
            pool.wait_ge(consts, 2)
            pool.affine_select(out=ident[:, :], in_=ident[:, :], compare_op=ALU.not_equal, fill=1.0, base=0,
                               pattern=[[-1, P]], channel_multiplier=1).then_inc(consts, 1)

        @block.scalar
        def _(act):
            for s in free_at_start["act"]:
                act.sem_inc(s, FREE)

            act.dma_start(cols[:, :], cols_d[:, :]).then_inc(cols_in, 16)
            for k in range(4):
                act.dma_start(x[:, 2 * k:2 * k + 2, :], xt[:, 2 * k:2 * k + 2, :]).then_inc(x_in[k], 16)
            act.dma_start(rs_bc[:, :], wst_d[:, :]).then_inc(ws_in, 16)
            act.dma_start(bs_bc[:, :], bs_d[:, :]).then_inc(bs_in, 16)

            def cut_hi(w, slot, land, first=False):
                act.wait_ge(landed[slot[1]], land)
                if not first:
                    act.wait_ge(blocks, 2 * w - (2 * LEAD - 1))
                act.activation(w_hi[:, slot[0], :], raw[:, slot[1], :], ACT.Copy).then_inc(hi_cut, 1)

            def cut_hi_late(n, s):
                w = s + LEAD
                cut_hi(4 * n + w, (w % 4, w % 4), 16 * (n + Q_MINUS_W // 4 + w // 4 + 1))

            def sqrt_var(k):
                act.wait_ge(var_ready, k + 1)
                act.activation(small[:, 1, :], small[:, 0, :], ACT.Sqrt).then_inc(sd_ready, 1)

            def make_h_hi(layer):
                for k in range(KD):
                    act.wait_ge(h_made, KD * layer + k + 1)
                    act.activation(h_hi[:, k, :], tmp[:, k % 2, :], ACT.Copy).then_inc(h_hi_cut, 1)

            act.wait_ge(cols_in, 16)
            act.activation(silu_c[:, :], cols[:, C_C:C_C + KD], ACT.Silu).then_inc(sc_ready, 1)
            for k in range(KD):
                act.wait_ge(x_in[k // 2], 16)
                if k >= 2:
                    act.wait_ge(sq_added, k - 1)
                act.activation(tmp[:, 2 + k % 2, :], x[:, k, :], ACT.Square).then_inc(sq_ready, 1)
            act.wait_ge(ws_in, 16)
            act.activation(ws_hi[:, :], rs_bc[:, :], ACT.Copy).then_inc(ws_hi_cut, 1)
            act.wait_ge(consts, 3)
            act.activation(ones_r[:, :], ones[:, :], ACT.Copy).then_inc(ws_hi_cut, 1)
            sqrt_var(0)
            make_h_hi(0)
            act.wait_ge(rs_summed, 1)
            for half in range(2):
                act.activation(rs_bc[:, half * S:(half + 1) * S], p_sv[half][:, :], ACT.Copy).then_inc(sv_used, 1)
            for w in range(LEAD):
                cut_hi(w, (w, (MOD_START + w) % 4), q_round(MOD_START + w), first=True)

            with act.Fori(0, PAIRS) as i:
                for s in range(8):
                    q = A_Q0 + A_W_AT[s]
                    cut_hi(8 * i + (s + LEAD), ((s + LEAD) % 4, q % 4), 48 * i + q_round(q))
                    if s == 2:
                        act.wait_ge(y_cut, 2 * i + FREE)
                        for u in range(2):
                            act.wait_ge(blocks, 16 * i + (2 + u + 1))
                            act.activation(tmp[:, 2 + u, :], pp[u][:, :], ACT.Copy).then_inc(cg_ready, 1)
                    if s == 6:
                        for u in range(2):
                            act.wait_ge(blocks, 16 * i + (10 + u + 1))
                            act.activation(tmp[:, u, :], pp[u][:, :], ACT.Silu).then_inc(sz_ready, 1)

            def square_x(layer, j):
                for u in range(2):
                    act.wait_ge(x_updated, 2 * j + ((KD + 1) * layer + FREE + u + 2))
                    act.wait_ge(sq_added, 2 * j + KD * (layer + 1))
                    act.activation(tmp[:, 2 + u, :], x[:, bass.ds(2 * j + u, 1), :], ACT.Square).then_inc(sq_ready, 1)

            with act.Fori(0, DPAIRS) as j:
                for s in range(4):
                    cut_hi_late(j + W_AOUT // 4, s)
                square_x(0, j)
            sqrt_var(1)
            make_h_hi(1)

            with act.Fori(0, 4) as c:
                for s in range(4):
                    cut_hi_late(c + W_BV // 4, s)
                act.wait_ge(v_cut, 4 * c + FREE)
                for st in range(NCH):
                    act.wait_ge(blocks, 8 * c + (2 * W_BV + 6 + st // 2 + 1))
                    act.activation(tmp[:, st, :], pp[st][:, :], ACT.Gelu).then_inc(v_gelu, 1)
            sqrt_var(2)

            with act.Fori(0, PAIRS) as i:
                for s in range(4):
                    cut_hi_late(i + W_BUZ // 4, s)
                    if s == 2:
                        act.wait_ge(y_cut, 2 * i + (KE + FREE))
                        for u in range(2):
                            act.wait_ge(blocks, 8 * i + (2 * W_BUZ + 2 + u + 1))
                            act.activation(tmp[:, 2 + u, :], pp[u][:, :], ACT.Gelu).then_inc(u_gelu, 1)
                for u in range(2):
                    act.wait_ge(blocks, 8 * i + (2 * W_BUZ + 6 + u + 1))
                    act.activation(tmp[:, u, :], pp[2 + u][:, :], ACT.Silu).then_inc(z_silu, 1)

            with act.Fori(0, DPAIRS - 1) as j:
                for s in range(4):
                    cut_hi_late(j + W_BOUT // 4, s)
                square_x(1, j)
            cut_hi_late(DPAIRS - 1 + W_BOUT // 4, 0)
            square_x(1, DPAIRS - 1)
            sqrt_var(3)

        @block.tensor
        def _(pe):
            for s in free_at_start["pe"]:
                pe.sem_inc(s, FREE)

            def unit_block(ring, u, bank, kts, rhs_hi, rhs_lo, first, last):
                for n, kt in enumerate(kts):
                    at = slice(256 * n + P * u, 256 * n + P * (u + 1))
                    pe.matmul(bank[:, :], w_hi[:, ring, at], rhs_hi[:, kt, :], start=first and n == 0, stop=False)
                    pe.matmul(bank[:, :], w_hi[:, ring, at], rhs_lo[:, kt, :], start=False, stop=False)
                    mm = pe.matmul(bank[:, :], w_lo[:, ring, at], rhs_hi[:, kt, :], start=False,
                                   stop=last and n == len(kts) - 1)
                mm.then_inc(blocks, 1)

            def mod_columns(g, buf, used):
                pe.wait_ge(consumed, used)
                for t in range(2):
                    mm = pe.matmul(p_small[:, g + t:g + t + 1], acc[:, buf, P * t:P * (t + 1)], ones[:, 0:1],
                                   start=True, stop=True)
                mm.then_inc(acc_used, 1)

            def norm_sums(k, added):
                pe.wait_ge(sq_added, added)
                for st in range(NCH):
                    mm = pe.matmul(p_rstd[:, st:st + 1], ssum[:, P * st:P * (st + 1)], ones[:, 0:1],
                                   start=True, stop=True)
                mm.then_inc(stat_sum, 1)

            def rstd_broadcast(k):
                pe.wait_ge(diag_ready, k + 1)
                pe.matmul(p_rstd[:, :], ones[:, :], work[:, 0, :], start=True, stop=True).then_inc(rstd_bc, 1)

            pe.wait_ge(consts, 3)
            for g in range(4):
                mod_columns((8, 0)[g % 2] + 2 * (g // 2), g % 2, 2 * (g + 1))
            norm_sums(0, KD)
            pe.wait_ge(ws_cut, 1)
            pe.wait_ge(ws_hi_cut, 2)
            for half in range(2):
                at = slice(half * S, (half + 1) * S)
                pe.matmul(p_sv[half][:, :], ones_r[:, :], ws_hi[:, at], start=True, stop=False)
                mm = pe.matmul(p_sv[half][:, :], ones_r[:, :], ws_lo[:, at], start=False, stop=True)
            mm.then_inc(rs_summed, 1)
            for g in range(4, 8):
                if g == 6:
                    rstd_broadcast(0)
                mod_columns((8, 0)[g % 2] + 2 * (g // 2), g % 2, 2 * (g + 1))

            with pe.Fori(0, PAIRS) as i:
                for s in range(8):
                    q = A_Q0 - 12 + A_W_AT[s + 8 - LEAD] if s < LEAD else A_Q0 + A_W_AT[s - LEAD]
                    pe.wait_ge(consumed, 12 * i + (q + 1))
                    if s == 0:
                        pe.wait_ge(sz_ready, 2 * i + FREE)
                    if s == 2:
                        pe.wait_ge(bg_used, 2 * i + FREE)
                    if s == 4:
                        pe.wait_ge(cg_ready, 2 * i + 2)
                    if s == 6:
                        pe.wait_ge(xh_used, 2 * i + 2)
                    if s < 2:
                        pe.wait_ge(h_cut, 4 * (s + 1))
                    for u in range(2):
                        unit_block(s % 4, u, pp[2 * (s // 2 % 2) + u], range(4 * (s % 2), 4 * (s % 2) + 4), h_hi, h_lo,
                                   s % 2 == 0, s % 2 == 1)
                    if s in (4, 6):
                        n = s // 2 - 2
                        mod_columns(2 * n, n, 12 * i + (A_Q0 + A_MOD_AT[2 * n + 1] + 1))

            def out_product(layer, w0, j):
                for s in range(4):
                    pe.wait_ge(consumed, 4 * j + (w0 + s + Q_MINUS_W + 1))
                    pe.wait_ge(y_cut, KE * layer + 4 * (s + 1) + FREE)
                    for u in range(2):
                        if s == 0:
                            pe.wait_ge(x_updated, 2 * j + ((KD + 1) * layer + FREE + u))
                        unit_block(s, u, pp[u], range(4 * s, 4 * s + 4), y_hi, y_lo, s == 0, s == 3)

            pe.wait_ge(sz_ready, KE + FREE)
            with pe.Fori(0, DPAIRS) as j:
                out_product(0, W_AOUT, j)
            norm_sums(1, 2 * KD)
            rstd_broadcast(1)

            def v_product(c, first):
                for s in range(4):
                    pe.wait_ge(consumed, 4 * c + (W_BV + s + Q_MINUS_W + 1))
                    for st in range(NCH):
                        if s == 0 and not first:
                            pe.wait_ge(v_gelu, 4 * c + (st - 3))
                        for n in range(2):
                            kt = 2 * s + n
                            if first and st == 0:
                                pe.wait_ge(h_cut, KD + kt + 1)
                            left_hi, left_lo = (a[:, kt, P * st:P * (st + 1)] for a in (h_hi, h_lo))
                            right_hi, right_lo = (a[:, s, S * n:S * (n + 1)] for a in (w_hi, w_lo))
                            pe.matmul(pp[st][:, :], left_hi, right_hi, start=kt == 0, stop=False)
                            pe.matmul(pp[st][:, :], left_hi, right_lo, start=False, stop=False)
                            mm = pe.matmul(pp[st][:, :], left_lo, right_hi, start=False, stop=kt == KD - 1)
                        if st % 2:
                            mm.then_inc(blocks, 1)

            pe.wait_ge(bg_used, KE + FREE)
            v_product(0, True)
            with pe.Fori(1, 4) as c:
                v_product(c, False)

            pe.wait_ge(v_gelu, 16)
            with pe.Fori(0, PAIRS) as i:
                for s in range(4):
                    pe.wait_ge(consumed, 4 * i + (W_BUZ + s + Q_MINUS_W + 1))
                    if s == 0:
                        pe.wait_ge(u_gelu, 2 * i + FREE)
                    if s == 2:
                        pe.wait_ge(z_silu, 2 * i + FREE)
                        pe.wait_ge(sv_used, 2 * i + 2)
                        for u in range(2):
                            for n in range(NCH):
                                pe.wait_ge(vn_cut, 4 * i + (n + 1))
                                at = slice(P * n, P * (n + 1))
                                right_hi, right_lo = (a[:, bass.ds(P * i, P)] for a in (ws_hi, ws_lo))
                                o = p_sv[u][:, at]
                                pe.matmul(o, vn_hi[:, u, at], right_hi, start=True, stop=False)
                                pe.matmul(o, vn_hi[:, u, at], right_lo, start=False, stop=False)
                                mm = pe.matmul(o, vn_lo[:, u, at], right_hi, start=False, stop=True)
                            mm.then_inc(sv_done, 1)
                    for u in range(2):
                        unit_block(s, u, pp[2 * (s // 2) + u], range(4 * (s % 2), 4 * (s % 2) + 4), h_hi, h_lo,
                                   s % 2 == 0, s % 2 == 1)

            pe.wait_ge(u_gelu, KE + FREE)
            with pe.Fori(0, DPAIRS) as j:
                out_product(1, W_BOUT, j)
            norm_sums(2, 3 * KD)
            rstd_broadcast(2)

        @block.vector
        def _(dve):
            for s in free_at_start["dve"]:
                dve.sem_inc(s, FREE)

            at = [0]

            def step(ins):
                ins.then_inc(dve_step, 1)
                at[0] = at[0] + 1
                return at[0]

            def after(n):
                dve.wait_ge(dve_step, n)

            def loop(n, steps, body):
                base = at[0]
                with dve.Fori(0, n) as i:
                    at[0] = i * steps + base
                    body(i)
                at[0] = base + n * steps

            def f32(ap):
                return ap.bitcast(F32)

            def cut_lo(n, slot):
                dve.wait_ge(hi_cut, n)
                dve.tensor_tensor(w_lo[:, slot[0], :], raw[:, slot[1], :], f32(w_hi[:, slot[0], :]),
                                  ALU.subtract).then_inc(consumed, 1)

            def cut_lo_late(n, s):
                w = s + LEAD
                cut_lo(4 * n + (w + 1), (w % 4, w % 4))

            def mod_slot(rq, land, half, buf, used, wait_acc=None):
                dve.wait_ge(landed[rq], land)
                if wait_acc is not None:
                    dve.wait_ge(acc_used, wait_acc)
                if half:
                    dve.wait_ge(consumed, used)
                for n in range(4):
                    kt = 4 * half + n
                    w = raw[:, rq, 256 * n:256 * (n + 1)]
                    a = acc[:, buf, :]
                    if kt == 0:
                        ins = dve.tensor_scalar(a, w, silu_c[:, kt:kt + 1], None, ALU.mult)
                    else:
                        if n:
                            after(at[0])
                        ins = dve.scalar_tensor_tensor(out=a, in0=w, scalar=silu_c[:, kt:kt + 1], in1=a,
                                                       op0=ALU.mult, op1=ALU.add)
                    if n < 3:
                        step(ins)
                    else:
                        ins.then_inc(consumed, 1)

            def add_square(n, buf):
                dve.wait_ge(sq_ready, n)
                dve.wait_ge(sq_added, n - 1)
                dve.tensor_tensor(ssum[:, :], ssum[:, :], tmp[:, buf, :], ALU.add).then_inc(sq_added, 1)

            def rsqrt(k, src, scale, dst):
                dve.tensor_scalar(small[:, 0, :], src, scale, EPS, ALU.mult, ALU.add).then_inc(var_ready, 1)
                dve.wait_ge(sd_ready, k + 1)
                after(step(dve.reciprocal(small[:, 2, :], small[:, 1, :])))
                after(step(dve.tensor_tensor(small[:, 3, :], small[:, 2, :], small[:, 2, :], ALU.mult)))
                after(step(dve.tensor_tensor(small[:, 3, :], small[:, 3, :], small[:, 0, :], ALU.mult)))
                after(step(dve.tensor_scalar(small[:, 3, :], small[:, 3, :], -0.5, 1.5, ALU.mult, ALU.add)))
                after(step(dve.tensor_tensor(dst, small[:, 2, :], small[:, 3, :], ALU.mult)))

            def rstd_diagonals(k, sqrt_no):
                dve.wait_ge(stat_sum, k + 1)
                rsqrt(sqrt_no, p_rstd[:, 0:NCH], 1.0 / D, small[:, 4, :])
                for st in range(NCH):
                    ins = dve.tensor_scalar(work[:, 0, P * st:P * (st + 1)], ident[:, :], small[:, 4, st:st + 1], None,
                                            ALU.mult)
                    if st < NCH - 1:
                        step(ins)
                ins.then_inc(diag_ready, 1)

            def make_h(layer):
                def low(k):
                    dve.wait_ge(h_hi_cut, KD * layer + k + 1)
                    dve.tensor_tensor(h_lo[:, k, :], tmp[:, k % 2, :], f32(h_hi[:, k, :]),
                                      ALU.subtract).then_inc(h_cut, 1)
                for k in range(KD):
                    if k >= 2:
                        dve.wait_ge(h_cut, KD * layer + k - 1)
                    after(step(dve.tensor_tensor(tmp[:, k % 2, :], x[:, k, :], p_rstd[:, :], ALU.mult)))
                    dve.tensor_scalar(tmp[:, k % 2, :], tmp[:, k % 2, :], amp[:, KD * layer + k:KD * layer + k + 1],
                                      mod[:, 3 * KD * layer + k:3 * KD * layer + k + 1],
                                      ALU.mult, ALU.add).then_inc(h_made, 1)
                    if k:
                        low(k - 1)
                low(KD - 1)

            def make_amp(layer):
                c = 3 * KD * layer + KD
                after(step(dve.scalar_tensor_tensor(
                    out=amp[:, KD * layer:KD * (layer + 1)], in0=mod[:, c:c + KD], scalar=1.0,
                    in1=cols[:, C_NORM + KD * layer:C_NORM + KD * (layer + 1)], op0=ALU.add, op1=ALU.mult)))

            after(step(dve.memset(ssum[:, :], 0.0)))
            dve.wait_ge(sc_ready, 1)
            for q in range(MOD_START):
                g = q // 2
                mod_slot(q % 4, q_round(q), q % 2, g % 2, q, g - 1 if g >= 2 and q % 2 == 0 else None)
                if 1 <= q <= KD:
                    add_square(q, 2 + (q - 1) % 2)
                if q == KD + 1:
                    dve.wait_ge(ws_hi_cut, 1)
                    dve.tensor_tensor(ws_lo[:, :], rs_bc[:, :], f32(ws_hi[:, :]), ALU.subtract).then_inc(ws_cut, 1)
                    rstd_diagonals(0, 0)
            dve.wait_ge(acc_used, 8)
            after(step(dve.tensor_tensor(mod[:, 0:2 * KD], p_small[:, 0:2 * KD], cols[:, C_BMOD:C_BMOD + 2 * KD],
                                         ALU.add)))
            make_amp(0)
            dve.wait_ge(rstd_bc, 1)
            make_h(0)
            for w in range(LEAD):
                cut_lo(w + 1, (w, (MOD_START + w) % 4))

            def layer_a(i):
                def mod_at(k):
                    q = A_Q0 + A_MOD_AT[k]
                    mod_slot(q % 4, 48 * i + q_round(q), k % 2, k // 2, 12 * i + q,
                             2 * i + (7 + k // 2) if k % 2 == 0 else None)

                def cut(s):
                    q = A_Q0 + A_W_AT[s]
                    cut_lo(8 * i + (s + LEAD + 1), ((s + LEAD) % 4, q % 4))

                mod_at(0)
                cut(0)
                cut(1)
                mod_at(1)
                cut(2)
                cut(3)
                mod_at(2)
                for u in range(2):
                    dve.wait_ge(cg_ready, 2 * i + (u + 1))
                    dve.wait_ge(blocks, 16 * i + (6 + u + 1))
                    dve.tensor_tensor(tmp[:, 2 + u, :], tmp[:, 2 + u, :], pp[2 + u][:, :],
                                      ALU.mult).then_inc(xh_used, 1)
                cut(4)

                def tap(t, u):
                    return cols[:, bass.ds(2 * i + (C_CONV + KE * t + u), 1)]

                n = []
                for u in range(2):
                    dve.wait_ge(xh_used, 2 * i + (u + 1))
                    n.append(step(dve.tensor_scalar(work[:, u, :], tmp[:, 2 + u, :], tap(1, u), None, ALU.mult)))
                for u in range(2):
                    after(n[u])
                    n[u] = step(dve.scalar_tensor_tensor(out=work[:, u, 1:S], in0=tmp[:, 2 + u, 0:S - 1],
                                                         scalar=tap(0, u), in1=work[:, u, 1:S],
                                                         op0=ALU.mult, op1=ALU.add))
                for u in range(2):
                    after(n[u])
                    n[u] = step(dve.scalar_tensor_tensor(out=work[:, u, 0:S - 1], in0=tmp[:, 2 + u, 1:S],
                                                         scalar=tap(2, u), in1=work[:, u, 0:S - 1],
                                                         op0=ALU.mult, op1=ALU.add))
                mod_at(3)
                cut(5)
                cut(6)
                for u in range(2):
                    after(n[u])
                    dve.wait_ge(sz_ready, 2 * i + (FREE + u + 1))
                    n[u] = step(dve.tensor_tensor(work[:, u, :], work[:, u, :], tmp[:, u, :], ALU.mult))
                dve.wait_ge(acc_used, 2 * i + 10)
                step(dve.tensor_tensor(mod[:, bass.ds(4 * i + 16, 4)], p_small[:, 0:4],
                                       cols[:, bass.ds(4 * i + (C_BMOD + 16), 4)], ALU.add))
                cut(7)
                for u in range(2):
                    after(n[u])
                    dve.wait_ge(blocks, 16 * i + (14 + u + 1))
                    dve.tensor_tensor(work[:, u, :], work[:, u, :], pp[2 + u][:, :], ALU.mult).then_inc(bg_used, 1)
                cut_y(i, bg_used, 2 * i + FREE)

            def cut_y(i, made, base):
                n = []
                for u in range(2):
                    dve.wait_ge(made, base + (u + 1))
                    n.append(step(dve.tensor_scalar(y_hi[:, bass.ds(2 * i + u, 1), :], work[:, u, :], 1.0, None, ALU.mult)))
                for u in range(2):
                    after(n[u])
                    dve.tensor_tensor(y_lo[:, bass.ds(2 * i + u, 1), :], work[:, u, :],
                                      f32(y_hi[:, bass.ds(2 * i + u, 1), :]), ALU.subtract).then_inc(y_cut, 1)

            loop(PAIRS, 4 * 3 + 3 * 2 + 2 + 1 + 2, layer_a)

            def update_x(layer, j):
                for u in range(2):
                    w = (W_AOUT, W_BOUT)[layer]
                    dve.wait_ge(blocks, 8 * j + (2 * w + 6 + u + 1))
                    xa = x[:, bass.ds(2 * j + u, 1), :]
                    dve.scalar_tensor_tensor(out=xa, in0=pp[u][:, :],
                                             scalar=mod[:, bass.ds(2 * j + (3 * KD * layer + 2 * KD + u), 1)], in1=xa,
                                             op0=ALU.mult, op1=ALU.add).then_inc(x_updated, 1)
                for u in range(2):
                    add_square(KD * (layer + 1) + 2 * j + (u + 1), 2 + u)

            def clear_ssum():
                dve.memset(ssum[:, :], 0.0).then_inc(x_updated, 1)

            dve.wait_ge(stat_sum, 1)
            clear_ssum()
            after(at[0])
            with dve.Fori(0, DPAIRS) as j:
                for s in range(4):
                    cut_lo_late(j + W_AOUT // 4, s)
                update_x(0, j)
            make_amp(1)
            rstd_diagonals(1, 1)
            dve.wait_ge(rstd_bc, 2)
            make_h(1)

            def layer_b_v(c):
                for s in range(4):
                    cut_lo_late(c + W_BV // 4, s)
                n = []
                for st in range(NCH):
                    dve.wait_ge(v_gelu, 4 * c + (st + 1))
                    step(dve.bn_stats(bstat[:, st, bass.ds(c, 1), :], tmp[:, st, :]))
                    n.append(step(dve.tensor_scalar(y_hi[:, bass.ds(4 * c, 4), P * st:P * (st + 1)],
                                                    tmp[:, st, :].rearrange("p (m e) -> p m e", e=P), 1.0, None,
                                                    ALU.mult)))
                    if st:
                        low(c, st - 1, n)
                low(c, NCH - 1, n)

            def low(c, st, n):
                after(n[st])
                dve.tensor_tensor(y_lo[:, bass.ds(4 * c, 4), P * st:P * (st + 1)],
                                  tmp[:, st, :].rearrange("p (m e) -> p m e", e=P),
                                  f32(y_hi[:, bass.ds(4 * c, 4), P * st:P * (st + 1)]),
                                  ALU.subtract).then_inc(v_cut, 1)

            loop(4, 2 * NCH, layer_b_v)

            for st in range(NCH):
                step(dve.bn_aggr(mv[:, st, :], bstat[:, st, :, :]))
            after(at[0])
            rsqrt(2, mv[:, :, 1], 1.0, small[:, 5, :])
            dve.wait_ge(bs_in, 16)
            dve.wait_ge(sv_used, 2)

            def layer_b_uz(i):
                cut_lo_late(i + W_BUZ // 4, 0)
                dve.wait_ge(v_cut, 16 + FREE)
                dve.wait_ge(sv_done, 2 * i + FREE)
                dve.wait_ge(y_cut, 2 * i + (KE + FREE))
                vt = work[:, :, :].rearrange("p a (b e) -> p a b e", e=P)
                n, k = [], []
                for st in range(NCH):
                    src_hi, src_lo = (a[:, bass.ds(2 * i, 2), P * st:P * (st + 1)] for a in (y_hi, y_lo))
                    n.append(step(dve.scalar_tensor_tensor(out=vt[:, :, st, :], in0=f32(src_hi),
                                                           scalar=mv[:, st, 0:1], in1=f32(src_lo),
                                                           op0=ALU.subtract, op1=ALU.add)))
                for st in range(NCH):
                    after(n[st])
                    k.append(step(dve.tensor_scalar(vn_hi[:, :, P * st:P * (st + 1)], vt[:, :, st, :],
                                                    small[:, 5, st:st + 1], None, ALU.mult)))
                cut_lo_late(i + W_BUZ // 4, 1)
                for st in range(NCH):
                    after(k[st])
                    dve.scalar_tensor_tensor(out=vn_lo[:, :, P * st:P * (st + 1)], in0=vt[:, :, st, :],
                                             scalar=small[:, 5, st:st + 1],
                                             in1=f32(vn_hi[:, :, P * st:P * (st + 1)]),
                                             op0=ALU.mult, op1=ALU.subtract).then_inc(vn_cut, 1)
                n = []
                for u in range(2):
                    n.append(step(dve.scalar_tensor_tensor(
                        out=term[:, u, :], in0=rs_bc[:, bass.ds(P * i, P)],
                        scalar=cols[:, bass.ds(2 * i + (C_LNB + u), 1)], in1=bs_bc[:, bass.ds(P * i, P)],
                        op0=ALU.mult, op1=ALU.add)))
                cut_lo_late(i + W_BUZ // 4, 2)
                dve.wait_ge(vn_cut, 4 * i + 4)
                for u in range(2):
                    dve.wait_ge(sv_done, 2 * i + (FREE + u + 1))
                    after(n[u])
                    tb = term[:, u, :].unsqueeze(1).broadcast_to([P, NCH, P])
                    dve.scalar_tensor_tensor(out=work[:, u, :].rearrange("p (b e) -> p b e", e=P),
                                             in0=p_sv[u][:, :].rearrange("p (b e) -> p b e", e=P),
                                             scalar=cols[:, bass.ds(2 * i + (C_LNG + u), 1)], in1=tb,
                                             op0=ALU.mult, op1=ALU.add).then_inc(sv_used, 1)
                n = []
                for u in range(2):
                    dve.wait_ge(sv_used, 2 * i + (2 + u + 1))
                    dve.wait_ge(u_gelu, 2 * i + (FREE + u + 1))
                    n.append(step(dve.tensor_tensor(work[:, u, :], work[:, u, :], tmp[:, 2 + u, :], ALU.mult)))
                cut_lo_late(i + W_BUZ // 4, 3)
                for u in range(2):
                    after(n[u])
                    dve.wait_ge(z_silu, 2 * i + (FREE + u + 1))
                    n[u] = step(dve.tensor_tensor(work[:, u, :], work[:, u, :], tmp[:, u, :], ALU.mult))
                cut_y(i, dve_step, n[0] - 1)

            loop(PAIRS, 4 + 4 + 2 + 2 + 2 + 2, layer_b_uz)

            dve.wait_ge(stat_sum, 2)
            clear_ssum()
            with dve.Fori(0, DPAIRS - 1) as j:
                for s in range(4):
                    cut_lo_late(j + W_BOUT // 4, s)
                update_x(1, j)
            cut_lo_late(DPAIRS - 1 + W_BOUT // 4, 0)
            update_x(1, DPAIRS - 1)

            rstd_diagonals(2, 3)
            dve.wait_ge(rstd_bc, 3)
            for k in range(KD):
                dve.scalar_tensor_tensor(out=x[:, k, :], in0=x[:, k, :], scalar=cols[:, C_FG + k:C_FG + k + 1],
                                         in1=p_rstd[:, :], op0=ALU.mult, op1=ALU.mult).then_inc(out_ready, 1)


def _slot(w, row, col, n_tiles, width):
    part = w[row:row + n_tiles * P, col:col + width].reshape(n_tiles, P, width)
    return part.transpose(1, 0, 2).reshape(P, n_tiles * width)


def _stream(w_mod, a_in, a_out, b_in, b_out):
    def mod_group(g, half):
        return _slot(w_mod[g // 12], 512 * half, 256 * (g % 12), 4, 256)

    w = []
    for i in range(PAIRS):
        for col in (2 * E, 3 * E, 0, E):
            w += [_slot(a_in, 512 * half, col + 256 * i, 4, 256) for half in range(2)]
    for j in range(DPAIRS):
        w += [_slot(a_out, 512 * s, 256 * j, 4, 256) for s in range(4)]
    for c in range(4):
        w += [_slot(b_in, 256 * s, 2 * E + 512 * c, 2, 512) for s in range(4)]
    for i in range(PAIRS):
        for col in (E, 0):
            w += [_slot(b_in, 512 * half, col + 256 * i, 4, 256) for half in range(2)]
    for j in range(DPAIRS):
        w += [_slot(b_out, 512 * s, 256 * j, 4, 256) for s in range(4)]
    q = [mod_group(g, half) for k in range(4) for g in (4 + k, k) for half in range(2)]
    q += w[:LEAD]
    for i in range(PAIRS):
        for what in A_ORDER:
            if isinstance(what, str):
                k = int(what[1])
                q.append(mod_group(8 + 2 * i + k // 2, k % 2))
            else:
                q.append(w[8 * i + LEAD + what])
    q += w[8 * PAIRS + LEAD:]
    return np.stack(q)


def kernel(x, c, norm_g, w_mod, b_mod, a_w_in, a_w_conv, a_w_out, b_w_in, b_ln_g, b_ln_b, b_w_s, b_b_s, b_w_out,
           final_g):
    import concourse.bacc as bacc
    from concourse.bass_utils import run_bass_kernel_spmd

    a = {k: np.asarray(v) for k, v in dict(x=x, c=c, norm_g=norm_g, w_mod=w_mod, b_mod=b_mod, a_w_in=a_w_in,
         a_w_conv=a_w_conv, a_w_out=a_w_out, b_w_in=b_w_in, b_ln_g=b_ln_g, b_ln_b=b_ln_b, b_w_s=b_w_s, b_b_s=b_b_s,
         b_w_out=b_w_out, final_g=final_g).items()}
    rows = [a["norm_g"], a["b_mod"], a["c"], a["b_ln_g"], a["b_ln_b"], a["final_g"], a["a_w_conv"][0].T]
    arrays = {
        "stream": _stream(a["w_mod"], a["a_w_in"][0], a["a_w_out"][0], a["b_w_in"][0], a["b_w_out"][0]),
        "xt": np.ascontiguousarray(a["x"][0].T.reshape(KD, P, S).transpose(1, 0, 2)),
        "cols": np.ascontiguousarray(np.concatenate([r.reshape(-1, P) for r in rows]).T),
        "wst": np.ascontiguousarray(a["b_w_s"][0].transpose(2, 0, 1).reshape(P, 8 * P)),
        "bs": np.ascontiguousarray(np.broadcast_to(a["b_b_s"][0].reshape(1, 8 * P), (P, 8 * P))),
    }
    nc = bacc.Bacc("TRN2", target_bir_lowering=False, num_devices=1)
    args = [nc.dram_tensor(f"in_{n}", v.shape, F32, kind="ExternalInput").ap() for n, v in arrays.items()]
    out = nc.dram_tensor("out_t", (KD, P, S), F32, kind="ExternalOutput").ap()
    build(nc, *args, out)
    r = run_bass_kernel_spmd(nc, [{f"in_{n}": v for n, v in arrays.items()}], core_ids=[0])
    return np.ascontiguousarray(r.results[0]["out_t"].reshape(D, S).T)[None]
```

```python
from contextlib import ExitStack

import numpy as np

import concourse.bass as bass
from concourse import mybir

F32 = mybir.dt.float32
F32R = mybir.dt.float32r
ACT = mybir.ActivationFunctionType
ALU = mybir.AluOpType

P = 128
D = 1024
S = 512
E = 2048
KD = D // P
KE = E // P
NCH = S // P
HALF = S // 2
EPS = 1e-6

SLOT = 1024
RING = 4
N_RSQRT = 6
X_STEPS = KD + 2 + 1
SQ_STEPS = KD + 2 + 1
SQ_START = KD + 1
FREE = 2
LEAD = 3
PAIRS = KE // 2
DPAIRS = KD // 2

W_AOUT = 8 * PAIRS
W_BV = W_AOUT + 4 * DPAIRS
W_BUZ = W_BV + 16
W_BOUT = W_BUZ + 4 * PAIRS
W_END = W_BOUT + 4 * DPAIRS
Q_END = 4 * DPAIRS + 4 * PAIRS + W_END
Q_MINUS_W = Q_END - W_END
START_ORDER = ["s0", "s0", "s0", "s0", 0, "s1", "s1", 2, "s1", "s1", 1, "s2", "s2", "s2", "s2", 3, "s3", "s3", 5, "s3",
               "s3", 4, "m0", 6, "m1", 7, "m2", "m3", 8, 9, 10]
S_AT = [[q for q, what in enumerate(START_ORDER) if what == f"s{kp}"] for kp in range(4)]
CUT_ORDER = [what for what in START_ORDER if not isinstance(what, str)]
Q_START = len(START_ORDER)
A_ORDER = ["m0", 0, 1, "m1", 2, 3, "m2", 4, "m3", 5, 6, 7]
A_MOD_AT = [A_ORDER.index(f"m{k}") for k in range(4)]
A_W_AT = [A_ORDER.index(k) for k in range(8)]
A_Q0 = Q_START - len(A_ORDER)

C_NORM = 0
C_BMOD = C_NORM + 2 * KD
C_C = C_BMOD + 6 * KD
C_LNG = C_C + KD
C_LNB = C_LNG + KE
C_FG = C_LNB + KE
C_CONV = C_FG + KD
N_COL = C_CONV + 3 * KE


def build(nc, stream, xt, cols_d, wst_d, bs_d, out):
    ctx = ExitStack()
    with ctx:
        def sb(name, shape, dt=F32):
            return ctx.enter_context(nc.sbuf_tensor(name, shape, dt))

        def sem(name):
            return ctx.enter_context(nc.semaphore(name))

        raw = sb("raw", [P, RING, SLOT])
        w_hi = sb("w_hi", [P, RING, SLOT], F32R)
        w_lo = sb("w_lo", [P, RING, SLOT], F32R)
        x = sb("x", [P, KD, S])
        h_hi = sb("h_hi", [P, KD, S], F32R)
        h_lo = sb("h_lo", [P, KD, S], F32R)
        y_hi = sb("y_hi", [P, KE, S], F32R)
        y_lo = sb("y_lo", [P, KE, S], F32R)
        ws_hi = sb("ws_hi", [P, 8 * P], F32R)
        ws_lo = sb("ws_lo", [P, 8 * P], F32R)
        vn_hi = sb("vn_hi", [P, 2, S], F32R)
        vn_lo = sb("vn_lo", [P, 2, S], F32R)
        rs_bc = sb("rs_bc", [P, 8 * P])
        bs_bc = sb("bs_bc", [P, 8 * P])
        tmp = sb("tmp", [P, 4, S])
        work = sb("work", [P, 2, S])
        ssum = sb("ssum", [P, S])
        term = sb("term", [P, 2, P])
        acc = sb("acc", [P, 2, S])
        cols = sb("cols", [P, N_COL])
        silu_c = sb("silu_c", [P, KD])
        mod = sb("mod", [P, 6 * KD])
        amp = sb("amp", [P, 2 * KD])
        small = sb("small", [P, 8, 4])
        bstat = sb("bstat", [P, NCH, 4, 6])
        mv = sb("mv", [P, NCH, 2])
        ident = sb("ident", [P, P])
        minus_half = sb("minus_half", [P, NCH])
        ones = sb("ones", [P, P])
        ones_r = sb("ones_r", [P, P], F32R)

        pp = [ctx.enter_context(nc.psum_tensor(f"pp{b}", [P, S], F32)) for b in range(4)]
        p_small = ctx.enter_context(nc.psum_tensor("p_small", [P, S], F32))
        p_rstd = ctx.enter_context(nc.psum_tensor("p_rstd", [P, S], F32))
        p_sv = [ctx.enter_context(nc.psum_tensor(f"p_sv{u}", [P, S], F32)) for u in range(2)]

        landed = [sem(f"landed{j}") for j in range(RING)]
        consumed = sem("consumed")
        hi_cut = sem("hi_cut")
        blocks = sem("blocks")
        cols_in, x_in, ws_in, bs_in = sem("cols_in"), [sem(f"x_in{k}") for k in range(4)], sem("ws_in"), sem("bs_in")
        consts = sem("consts")
        sc_ready = sem("sc_ready")
        acc_used = sem("acc_used")
        ws_hi_cut, ws_cut = sem("ws_hi_cut"), sem("ws_cut")
        rs_summed = sem("rs_summed")
        sq_ready = sem("sq_ready")
        sq_added = sem("sq_added")
        stat_sum, var_ready, power_ready = sem("stat_sum"), sem("var_ready"), sem("power_ready")
        half_done = sem("half_done")
        diag_ready, rstd_bc = sem("diag_ready"), sem("rstd_bc")
        amp_ready = sem("amp_ready")
        h_scaled = sem("h_scaled")
        h_made, h_hi_cut, h_cut = sem("h_made"), sem("h_hi_cut"), sem("h_cut")
        cg_ready, xh_used, sz_ready, bg_used = sem("cg_ready"), sem("xh_used"), sem("sz_ready"), sem("bg_used")
        y_cut = sem("y_cut")
        x_updated = sem("x_updated")
        v_gelu, v_cut = sem("v_gelu"), sem("v_cut")
        u_gelu = sem("u_gelu")
        vn_cut, sv_done, sv_used = sem("vn_cut"), sem("sv_done"), sem("sv_used")
        z_silu = sem("z_silu")
        out_ready, out_sent = sem("out_ready"), sem("out_sent")
        dve_step = sem("dve_step")

        def q_round(q):
            return 16 * (q // RING + 1)

        ALL = slice(0, S)
        halves = [slice(0, HALF), slice(HALF, S)]
        p_half = [p_rstd, p_sv[0]]

        free_at_start = {"act": [sz_ready, u_gelu, z_silu], "pe": [sv_done, blocks], "dve": [bg_used, y_cut, x_updated, v_cut]}

        block = ctx.enter_context(nc.Block())

        @block.sync
        def _(sp):
            for k in range(4):
                sp.dma_start(x[:, 2 * k:2 * k + 2, :], xt[:, 2 * k:2 * k + 2, :]).then_inc(x_in[k], 16)
            for q in range(RING):
                sp.dma_start(raw[:, q, :], stream[q, :, :]).then_inc(landed[q], 16)
            with sp.Fori(1, Q_END // RING) as r:
                for j in range(RING):
                    sp.wait_ge(consumed, RING * r + (j - RING + 1))
                    sp.dma_start(raw[:, j, :], stream[RING * r + j, :, :]).then_inc(landed[j], 16)
            for n in range(KD):
                half, k = n // DPAIRS, 2 * (n % DPAIRS)
                sp.wait_ge(out_ready, 2 * n + 2)
                at = slice(HALF * half, HALF * (half + 1))
                sp.dma_start(out[:, k:k + 2, at], x[:, k:k + 2, at]).then_inc(out_sent, 16)
            sp.wait_ge(out_sent, 16 * KD)

        @block.gpsimd
        def _(pool):
            pool.memset(ident[:, :], 0.0).then_inc(consts, 1)
            pool.memset(ones[:, :], 1.0).then_inc(consts, 1)
            pool.wait_ge(consts, 2)
            pool.affine_select(out=ident[:, :], in_=ident[:, :], compare_op=ALU.not_equal, fill=1.0, base=0,
                               pattern=[[-1, P]], channel_multiplier=1).then_inc(consts, 1)
            pool.memset(minus_half[:, :], -0.5).then_inc(consts, 1)
            pool.wait_ge(consts, 4)
            for k in range(N_RSQRT):
                pool.wait_ge(var_ready, k + 1)
                pool.tensor_tensor(small[:, 2, :], small[:, 0, :], minus_half[:, :], ALU.pow).then_inc(power_ready, 1)
                if k in (0, 2):
                    pool.wait_ge(stat_sum, k + 1)
                    pool.memset(ssum[:, :], 0.0).then_inc(sq_added, 1)

        @block.scalar
        def _(act):
            for s in free_at_start["act"]:
                act.sem_inc(s, FREE)

            act.dma_start(cols[:, :], cols_d[:, :]).then_inc(cols_in, 16)

            def cut_hi(w, slot, land, first=False):
                act.wait_ge(landed[slot[1]], land)
                if not first:
                    act.wait_ge(blocks, 2 * w - (2 * LEAD - FREE))
                act.activation(w_hi[:, slot[0], :], raw[:, slot[1], :], ACT.Copy).then_inc(hi_cut, 1)

            def cut_hi_start(w):
                q = START_ORDER.index(w)
                cut_hi(w, (w % 4, q % 4), q_round(q), first=w < LEAD)

            def cut_hi_late(n, s):
                w = s + LEAD
                cut_hi(4 * n + w, (w % 4, w % 4), 16 * (n + Q_MINUS_W // 4 + w // 4 + 1))

            def h_pair(layer, done, kp, at):
                for k in (2 * kp, 2 * kp + 1):
                    act.wait_ge(h_scaled, done + k + 1)
                    act.activation(tmp[:, k % 4, at], tmp[:, k % 4, at], ACT.Identity,
                                   scale=amp[:, KD * layer + k:KD * layer + k + 1],
                                   bias=mod[:, 3 * KD * layer + k:3 * KD * layer + k + 1]).then_inc(h_made, 1)
                    act.wait_ge(h_made, done + k + 1)
                    act.activation(h_hi[:, k, at], tmp[:, k % 4, at], ACT.Copy).then_inc(h_hi_cut, 1)

            for k in range(KD):
                act.wait_ge(x_in[k // 2], 16)
                if k >= 4:
                    act.wait_ge(sq_added, k - 2)
                act.activation(tmp[:, k % 4, :], x[:, k, :], ACT.Square).then_inc(sq_ready, 1)
                if k == 1:
                    act.wait_ge(cols_in, 16)
                    act.activation(silu_c[:, :], cols[:, C_C:C_C + KD], ACT.Silu).then_inc(sc_ready, 1)
            for kp, before, after in ((0, [0], [2]), (1, [1], []), (2, [3], [5]), (3, [4], [6])):
                for w in before:
                    cut_hi_start(w)
                act.wait_ge(amp_ready, kp + 1)
                h_pair(0, 0, kp, ALL)
                for w in after:
                    cut_hi_start(w)
            act.dma_start(rs_bc[:, :], wst_d[:, :]).then_inc(ws_in, 16)
            act.dma_start(bs_bc[:, :], bs_d[:, :]).then_inc(bs_in, 16)
            for u in range(2):
                act.wait_ge(blocks, FREE + 9)
                act.wait_ge(h_cut, KD)
                act.activation(tmp[:, 2 + u, :], pp[u][:, :], ACT.Copy).then_inc(cg_ready, 1)
            cut_hi_start(7)
            cut_hi_start(8)
            for u in range(2):
                act.wait_ge(blocks, FREE + 10 + u + 1)
                act.activation(tmp[:, u, :], p_sv[u][:, :], ACT.Silu).then_inc(sz_ready, 1)
            cut_hi_start(9)
            cut_hi_start(10)

            with act.Fori(1, PAIRS) as i:
                for s in range(8):
                    q = A_Q0 + A_W_AT[s]
                    cut_hi(8 * i + (s + LEAD), ((s + LEAD) % 4, q % 4), 48 * i + q_round(q))
                    if s == 2:
                        act.wait_ge(y_cut, 2 * i + FREE)
                        for u in range(2):
                            act.wait_ge(blocks, 16 * i + (FREE + 2 + u + 1))
                            act.activation(tmp[:, 2 + u, :], pp[u][:, :], ACT.Copy).then_inc(cg_ready, 1)
                    if s == 6:
                        for u in range(2):
                            act.wait_ge(blocks, 16 * i + (FREE + 10 + u + 1))
                            act.activation(tmp[:, u, :], pp[u][:, :], ACT.Silu).then_inc(sz_ready, 1)

            def square_x(layer, j):
                for u in range(2):
                    act.wait_ge(x_updated, 2 * j + (X_STEPS * layer + FREE + u + 2))
                    act.wait_ge(sq_added, 2 * j + (SQ_START + SQ_STEPS * layer + 1))
                    act.activation(tmp[:, 2 + u, :], x[:, bass.ds(2 * j + u, 1), :], ACT.Square).then_inc(sq_ready, 1)

            def square_half(layer, half):
                for u in range(2):
                    act.wait_ge(x_updated, X_STEPS * layer + FREE + 1 + 6 + 2 * half + u + 1)
                    if half == 1:
                        act.wait_ge(sq_added, SQ_START + SQ_STEPS * layer + 1 + 6 + 2)
                    act.activation(work[:, 1, HALF * u:HALF * (u + 1)], x[:, 6 + u, halves[half]],
                                   ACT.Square).then_inc(sq_ready, 1)

            act.wait_ge(ws_in, 16)
            act.activation(ws_hi[:, :], rs_bc[:, :], ACT.Copy).then_inc(ws_hi_cut, 1)
            act.wait_ge(consts, 3)
            act.activation(ones_r[:, :], ones[:, :], ACT.Copy).then_inc(ws_hi_cut, 1)
            with act.Fori(0, DPAIRS - 1) as j:
                for s in range(4):
                    cut_hi_late(j + W_AOUT // 4, s)
                square_x(0, j)
            act.wait_ge(rs_summed, 1)
            for n in range(2):
                act.activation(rs_bc[:, n * S:(n + 1) * S], p_sv[n][:, :], ACT.Copy).then_inc(sv_used, 1)
            last = W_AOUT // 4 + DPAIRS - 1
            cut_hi_late(last, 0)
            square_half(0, 0)
            for s in range(1, 4):
                cut_hi_late(last, s)
            h_pair(1, KD, 0, halves[0])
            h_pair(1, KD, 1, halves[0])
            square_half(0, 1)
            cut_hi_late(W_BV // 4, 0)
            h_pair(1, KD, 2, halves[0])
            h_pair(1, KD, 3, halves[0])
            for kp in range(4):
                h_pair(1, 2 * KD, kp, halves[1])

            def v_gelus(c, sts, wait):
                for st in sts:
                    act.wait_ge(*wait(st))
                    act.activation(tmp[:, st, :], pp[st][:, :], ACT.Gelu).then_inc(v_gelu, 1)

            act.wait_ge(h_cut, 3 * KD)
            v_gelus(0, (0, 1), lambda st: (half_done, 3))
            for s in range(1, 4):
                cut_hi_late(W_BV // 4, s)
            v_gelus(0, (2, 3), lambda st: (blocks, FREE + 2 * W_BV + 6 + st - 1))
            with act.Fori(1, 4) as c:
                for s in range(4):
                    cut_hi_late(c + W_BV // 4, s)
                act.wait_ge(v_cut, 4 * c + FREE)
                v_gelus(c, range(NCH), lambda st: (blocks, 8 * c + (FREE + 2 * W_BV + 6 + st // 2 + 1)))

            with act.Fori(0, PAIRS) as i:
                for s in range(4):
                    cut_hi_late(i + W_BUZ // 4, s)
                    if s == 2:
                        act.wait_ge(v_cut, 16 + FREE)
                        act.wait_ge(y_cut, 2 * i + (KE + FREE))
                        for u in range(2):
                            act.wait_ge(blocks, 8 * i + (FREE + 2 * W_BUZ + 2 + u + 1))
                            act.activation(tmp[:, 2 + u, :], pp[u][:, :], ACT.Gelu).then_inc(u_gelu, 1)
                for u in range(2):
                    act.wait_ge(blocks, 8 * i + (FREE + 2 * W_BUZ + 6 + u + 1))
                    act.activation(tmp[:, u, :], pp[2 + u][:, :], ACT.Silu).then_inc(z_silu, 1)

            with act.Fori(0, DPAIRS - 1) as j:
                for s in range(4):
                    cut_hi_late(j + W_BOUT // 4, s)
                square_x(1, j)
            cut_hi_late(W_BOUT // 4 + DPAIRS - 1, 0)
            square_half(1, 0)
            square_half(1, 1)

        @block.tensor
        def _(pe):
            for s in free_at_start["pe"]:
                pe.sem_inc(s, FREE)

            def unit(out, stationary, rhs_hi, rhs_lo, kts, first, last):
                for n, kt in enumerate(kts):
                    hi, lo = stationary(n)
                    pe.matmul(out, hi, rhs_hi(kt), start=first and n == 0, stop=False)
                    pe.matmul(out, hi, rhs_lo(kt), start=False, stop=False)
                    mm = pe.matmul(out, lo, rhs_hi(kt), start=False, stop=last and n == len(kts) - 1)
                return mm

            def weights(ring, u, width=256):
                return lambda n: tuple(a[:, ring, width * n + P * u:width * n + P * (u + 1)] for a in (w_hi, w_lo))

            def rows(a, at=ALL):
                return lambda kt: a[:, kt, at]

            def mod_columns(pairs, used):
                pe.wait_ge(consumed, used)
                for col, parts in pairs:
                    for n, part in enumerate(parts):
                        mm = pe.matmul(p_small[:, col:col + 1], part, ones[:, 0:1], start=n == 0,
                                       stop=n == len(parts) - 1)
                mm.then_inc(acc_used, 1)

            def group_columns(n, used):
                mod_columns([(2 * n + t, [acc[:, n, P * t:P * (t + 1)]]) for t in range(2)], used)

            def half_sums(half, added):
                pe.wait_ge(sq_added, added)
                for st in range(2):
                    at = slice(HALF * half + P * st, HALF * half + P * (st + 1))
                    mm = pe.matmul(p_half[half][:, st:st + 1], ssum[:, at], ones[:, 0:1], start=True, stop=True)
                mm.then_inc(stat_sum, 1)

            def broadcast(out, n, at):
                pe.wait_ge(diag_ready, n)
                pe.matmul(out, ones[:, :], work[:, 0, at], start=True, stop=True).then_inc(rstd_bc, 1)

            def start_columns(kp):
                mod_columns([(4 * kp + t, [acc[:, kp % 2, P * t:P * (t + 1)]]) for t in range(4)], S_AT[kp][3] + 1)

            pe.wait_ge(consts, 3)
            pe.wait_ge(sq_added, 1 + KD)
            for st in range(NCH):
                mm = pe.matmul(p_rstd[:, st:st + 1], ssum[:, P * st:P * (st + 1)], ones[:, 0:1], start=True, stop=True)
            mm.then_inc(stat_sum, 1)
            broadcast(p_rstd[:, :], 1, ALL)
            start_columns(0)
            for kp in range(4):
                w = (0, 1, 3, 4)[kp]
                pe.wait_ge(consumed, START_ORDER.index(w) + 1)
                for n in range(2):
                    k = 2 * kp + n
                    pe.wait_ge(h_cut, k + 1)
                    for b in range(2):
                        for u in range(2):
                            at = slice(S * n + P * (2 * b + u), S * n + P * (2 * b + u + 1))
                            mm = unit(pp[2 * b + u][:, :], lambda _: (w_hi[:, w % 4, at], w_lo[:, w % 4, at]),
                                      rows(h_hi), rows(h_lo), (k,), k == 0, k == KD - 1)
                        if n == 1:
                            mm.then_inc(blocks, 1)
                if kp < 3:
                    start_columns(kp + 1)
                w = (2, 5)[kp // 2]
                pe.wait_ge(consumed, START_ORDER.index(w) + 1)
                for u in range(2):
                    for n in range(2):
                        k = 2 * kp + n
                        at = slice(256 * (k % 4) + P * u, 256 * (k % 4) + P * (u + 1))
                        mm = unit(p_sv[u][:, :], lambda _: (w_hi[:, w % 4, at], w_lo[:, w % 4, at]),
                                  rows(h_hi), rows(h_lo), (k,), k == 0, k == KD - 1)
                    if kp % 2:
                        mm.then_inc(blocks, 1)
            pe.wait_ge(xh_used, 2)
            for w in (6, 7):
                pe.wait_ge(consumed, START_ORDER.index(w) + 1)
                for u in range(2):
                    unit(pp[2 + u][:, :], weights(w % 4, u), rows(h_hi), rows(h_lo), range(4 * (w - 6), 4 * (w - 5)),
                         w == 6, w == 7).then_inc(blocks, 1)
            for n in range(2):
                group_columns(n, START_ORDER.index(f"m{2 * n + 1}") + 1)
            pe.wait_ge(sz_ready, 2 + FREE)

            with pe.Fori(1, PAIRS) as i:
                for s in range(8):
                    q = A_Q0 - 12 + A_W_AT[s + 8 - LEAD] if s < LEAD else A_Q0 + A_W_AT[s - LEAD]
                    pe.wait_ge(consumed, 12 * i + (q + 1))
                    if s == 0:
                        pe.wait_ge(sz_ready, 2 * i + FREE)
                    if s == 2:
                        pe.wait_ge(bg_used, 2 * i + FREE)
                    if s == 4:
                        pe.wait_ge(cg_ready, 2 * i + 2)
                    if s == 6:
                        pe.wait_ge(xh_used, 2 * i + 2)
                    for u in range(2):
                        unit(pp[2 * (s // 2 % 2) + u][:, :], weights(s % 4, u), rows(h_hi), rows(h_lo),
                             range(4 * (s % 2), 4 * (s % 2) + 4), s % 2 == 0, s % 2 == 1).then_inc(blocks, 1)
                    if s in (4, 6):
                        n = s // 2 - 2
                        group_columns(n, 12 * i + (A_Q0 + A_MOD_AT[2 * n + 1] + 1))

            def out_slot(layer, w0, j, s):
                pe.wait_ge(consumed, 4 * j + (w0 + s + Q_MINUS_W + 1))
                pe.wait_ge(y_cut, KE * layer + 4 * (s + 1) + FREE)

            def out_product(layer, w0, j):
                for s in range(4):
                    out_slot(layer, w0, j, s)
                    for u in range(2):
                        if s == 0:
                            pe.wait_ge(x_updated, 2 * j + (X_STEPS * layer + FREE + u))
                        unit(pp[u][:, :], weights(s, u), rows(y_hi), rows(y_lo), range(4 * s, 4 * s + 4), s == 0,
                             s == 3).then_inc(blocks, 1)

            def last_out_product(layer, w0):
                for half in range(2):
                    for s in range(4):
                        out_slot(layer, w0, DPAIRS - 1, s)
                        for u in range(2):
                            if s == 0 and half == 0:
                                pe.wait_ge(x_updated, X_STEPS * layer + FREE + 6 + u)
                            mm = unit(pp[2 * half + u][:, 0:HALF], weights(s, u), rows(y_hi, halves[half]),
                                      rows(y_lo, halves[half]), range(4 * s, 4 * s + 4), s == 0, s == 3)
                            if half == 1:
                                mm.then_inc(blocks, 1)
                            elif s == 3 and u == 1:
                                mm.then_inc(half_done, 1)
                            if half == 1 and s == 1 and u == 0:
                                half_sums(0, SQ_START + SQ_STEPS * layer + 1 + 6 + 2)
                            if half == 1 and s == 2 and u == 1:
                                broadcast(p_half[0][:, 0:HALF], 2 * layer + 2, slice(0, HALF))

            pe.wait_ge(sz_ready, KE + FREE)
            with pe.Fori(0, DPAIRS - 1) as j:
                out_product(0, W_AOUT, j)
            pe.wait_ge(ws_cut, 1)
            pe.wait_ge(ws_hi_cut, 2)
            for n in range(2):
                at = slice(n * S, (n + 1) * S)
                pe.matmul(p_sv[n][:, :], ones_r[:, :], ws_hi[:, at], start=True, stop=False)
                mm = pe.matmul(p_sv[n][:, :], ones_r[:, :], ws_lo[:, at], start=False, stop=True)
            mm.then_inc(rs_summed, 1)
            pe.wait_ge(bg_used, KE + FREE)
            pe.wait_ge(sv_used, 2)
            last_out_product(0, W_AOUT)

            def v_tile(st, s, n):
                kt = 2 * s + n
                left_hi, left_lo = (a[:, kt, P * st:P * (st + 1)] for a in (h_hi, h_lo))
                right_hi, right_lo = (a[:, s, S * n:S * (n + 1)] for a in (w_hi, w_lo))
                pe.matmul(pp[st][:, :], left_hi, right_hi, start=kt == 0, stop=False)
                pe.matmul(pp[st][:, :], left_hi, right_lo, start=False, stop=False)
                return pe.matmul(pp[st][:, :], left_lo, right_hi, start=False, stop=kt == KD - 1)

            for half in range(2):
                if half == 0:
                    pe.wait_ge(x_updated, X_STEPS + FREE - 2)
                else:
                    pe.wait_ge(x_updated, X_STEPS + FREE)
                for s in range(4):
                    pe.wait_ge(consumed, W_BV + s + Q_MINUS_W + 1)
                    for n in range(2):
                        pe.wait_ge(h_cut, KD * (1 + half) + 2 * s + n + 1)
                        for st in (2 * half, 2 * half + 1):
                            mm = v_tile(st, s, n)
                            if half == 1 and n == 1:
                                mm.then_inc(blocks, 1)
                    if half == 0 and s == 1:
                        half_sums(1, SQ_START + 1 + 6 + 4)
                    if half == 0 and s == 2:
                        broadcast(p_half[1][:, 0:HALF], 3, slice(HALF, S))
                if half == 0:
                    mm.then_inc(half_done, 2)
            with pe.Fori(1, 4) as c:
                for s in range(4):
                    pe.wait_ge(consumed, 4 * c + (W_BV + s + Q_MINUS_W + 1))
                    for st in range(NCH):
                        if s == 0:
                            pe.wait_ge(v_gelu, 4 * c + (st - 3))
                        for n in range(2):
                            mm = v_tile(st, s, n)
                        if st % 2:
                            mm.then_inc(blocks, 1)

            pe.wait_ge(v_gelu, 16)
            with pe.Fori(0, PAIRS) as i:
                for s in range(4):
                    pe.wait_ge(consumed, 4 * i + (W_BUZ + s + Q_MINUS_W + 1))
                    if s == 0:
                        pe.wait_ge(u_gelu, 2 * i + FREE)
                    if s == 2:
                        pe.wait_ge(z_silu, 2 * i + FREE)
                        pe.wait_ge(sv_used, 2 * i + 2)
                        for u in range(2):
                            for n in range(NCH):
                                pe.wait_ge(vn_cut, 4 * i + (n + 1))
                                at = slice(P * n, P * (n + 1))
                                right_hi, right_lo = (a[:, bass.ds(P * i, P)] for a in (ws_hi, ws_lo))
                                o = p_sv[u][:, at]
                                pe.matmul(o, vn_hi[:, u, at], right_hi, start=True, stop=False)
                                pe.matmul(o, vn_hi[:, u, at], right_lo, start=False, stop=False)
                                mm = pe.matmul(o, vn_lo[:, u, at], right_hi, start=False, stop=True)
                            mm.then_inc(sv_done, 1)
                    for u in range(2):
                        unit(pp[2 * (s // 2) + u][:, :], weights(s, u), rows(h_hi), rows(h_lo),
                             range(4 * (s % 2), 4 * (s % 2) + 4), s % 2 == 0, s % 2 == 1).then_inc(blocks, 1)

            pe.wait_ge(u_gelu, KE + FREE)
            with pe.Fori(0, DPAIRS - 1) as j:
                out_product(1, W_BOUT, j)
            pe.wait_ge(z_silu, KE + FREE)
            pe.wait_ge(sv_used, 2 + KE)
            last_out_product(1, W_BOUT)
            half_sums(1, SQ_START + SQ_STEPS + 1 + 6 + 4)
            broadcast(p_half[1][:, 0:HALF], 5, slice(HALF, S))

        @block.vector
        def _(dve):
            for s in free_at_start["dve"]:
                dve.sem_inc(s, FREE)
            at = [0]

            def step(ins):
                ins.then_inc(dve_step, 1)
                at[0] = at[0] + 1
                return at[0]

            def after(n):
                dve.wait_ge(dve_step, n)

            def loop(start, end, steps, body):
                base = at[0]
                with dve.Fori(start, end) as i:
                    at[0] = i * steps + (base - start * steps)
                    body(i)
                at[0] = base + (end - start) * steps

            def f32(ap):
                return ap.bitcast(F32)

            def cut_lo(n, slot):
                dve.wait_ge(hi_cut, n)
                dve.tensor_tensor(w_lo[:, slot[0], :], raw[:, slot[1], :], f32(w_hi[:, slot[0], :]),
                                  ALU.subtract).then_inc(consumed, 1)

            def cut_lo_start(w):
                cut_lo(CUT_ORDER.index(w) + 1, (w % 4, START_ORDER.index(w) % 4))

            def cut_lo_late(n, s):
                w = s + LEAD
                cut_lo(4 * n + (w + 1), (w % 4, w % 4))

            def start_slot(kp, j):
                q = S_AT[kp][j]
                a = acc[:, kp % 2, :]
                dve.wait_ge(landed[q % 4], q_round(q))
                if j:
                    dve.wait_ge(consumed, S_AT[kp][j - 1] + 1)
                for n in range(2):
                    kt = 2 * j + n
                    w = raw[:, q % 4, S * n:S * (n + 1)]
                    if kt == 0:
                        ins = dve.tensor_scalar(a, w, silu_c[:, kt:kt + 1], None, ALU.mult)
                    else:
                        if n:
                            after(at[0])
                        ins = dve.scalar_tensor_tensor(out=a, in0=w, scalar=silu_c[:, kt:kt + 1], in1=a,
                                                       op0=ALU.mult, op1=ALU.add)
                    if n == 0:
                        step(ins)
                    else:
                        ins.then_inc(consumed, 1)

            def mod_slot(rq, land, half, buf, used, wait_acc=None):
                dve.wait_ge(landed[rq], land)
                if wait_acc is not None:
                    dve.wait_ge(acc_used, wait_acc)
                if half:
                    dve.wait_ge(consumed, used)
                for n in range(4):
                    kt = 4 * half + n
                    w = raw[:, rq, 256 * n:256 * (n + 1)]
                    a = acc[:, buf, 0:256]
                    if kt == 0:
                        ins = dve.tensor_scalar(a, w, silu_c[:, kt:kt + 1], None, ALU.mult)
                    else:
                        if n:
                            after(at[0])
                        ins = dve.scalar_tensor_tensor(out=a, in0=w, scalar=silu_c[:, kt:kt + 1], in1=a,
                                                       op0=ALU.mult, op1=ALU.add)
                    if n < 3:
                        step(ins)
                    else:
                        ins.then_inc(consumed, 1)

            def add_squares(layer, n, src, where):
                dve.wait_ge(sq_ready, n + (KD + (SQ_STEPS - 1) * layer))
                dve.wait_ge(sq_added, n + (SQ_START + SQ_STEPS * layer))
                dve.tensor_tensor(ssum[:, where], ssum[:, where], src, ALU.add).then_inc(sq_added, 1)

            def rsqrt(k, src, scale, n):
                dve.tensor_scalar(small[:, 0, 0:n], src, scale, EPS, ALU.mult, ALU.add).then_inc(var_ready, 1)

            def diagonals(k, n, first):
                dve.wait_ge(power_ready, k)
                for st in range(n):
                    ins = dve.tensor_scalar(work[:, 0, P * (first + st):P * (first + st + 1)], ident[:, :],
                                            small[:, 2, st:st + 1], None, ALU.mult)
                    if st < n - 1:
                        step(ins)
                ins.then_inc(diag_ready, 1)

            def scale_pair(done, kp, rstd, where):
                for k in (2 * kp, 2 * kp + 1):
                    dve.tensor_tensor(tmp[:, k % 4, where], x[:, k, where], rstd, ALU.mult).then_inc(h_scaled, 1)

            def cut_h_pair(done, kp, where):
                for k in (2 * kp, 2 * kp + 1):
                    dve.wait_ge(h_hi_cut, done + k + 1)
                    dve.tensor_tensor(h_lo[:, k, where], tmp[:, k % 4, where], f32(h_hi[:, k, where]),
                                      ALU.subtract).then_inc(h_cut, 1)

            dve.memset(ssum[:, :], 0.0).then_inc(sq_added, 1)
            for k in range(KD):
                dve.wait_ge(sq_ready, k + 1)
                dve.wait_ge(sq_added, k + 1)
                dve.tensor_tensor(ssum[:, :], ssum[:, :], tmp[:, k % 4, :], ALU.add).then_inc(sq_added, 1)
            dve.wait_ge(sc_ready, 1)
            start_slot(0, 0)
            dve.wait_ge(stat_sum, 1)
            rsqrt(1, p_rstd[:, 0:NCH], 1.0 / D, NCH)
            start_slot(0, 1)
            diagonals(1, NCH, 0)
            start_slot(0, 2)
            start_slot(0, 3)
            dve.wait_ge(rstd_bc, 1)
            scale_pair(0, 0, p_rstd[:, :], ALL)
            for kp in range(4):
                if kp < 3:
                    if kp:
                        dve.wait_ge(h_cut, 2 * kp)
                    cut_lo_start((0, 1, 3)[kp])
                    scale_pair(0, kp + 1, p_rstd[:, :], ALL)
                    start_slot(kp + 1, 0)
                else:
                    cut_lo_start(4)
                dve.wait_ge(acc_used, kp + 1)
                k = 2 * kp
                n = step(dve.scalar_tensor_tensor(out=amp[:, k:k + 2], in0=p_small[:, 4 * kp:4 * kp + 2], scalar=1.0,
                                                  in1=cols[:, C_BMOD + KD + k:C_BMOD + KD + k + 2],
                                                  op0=ALU.add, op1=ALU.add))
                m = step(dve.tensor_tensor(mod[:, k:k + 2], p_small[:, 4 * kp + 2:4 * kp + 4],
                                           cols[:, C_BMOD + k:C_BMOD + k + 2], ALU.add))
                after(m)
                dve.tensor_tensor(amp[:, k:k + 2], amp[:, k:k + 2], cols[:, C_NORM + k:C_NORM + k + 2],
                                  ALU.mult).then_inc(amp_ready, 1)
                if kp < 3:
                    start_slot(kp + 1, 1)
                cut_h_pair(0, kp, ALL)
                if kp < 3:
                    if kp != 1:
                        cut_lo_start((2, None, 5)[kp])
                    start_slot(kp + 1, 2)
                    start_slot(kp + 1, 3)

            def group_slot(i, k):
                if isinstance(i, int):
                    q = START_ORDER.index(f"m{k}")
                    mod_slot(q % 4, q_round(q), k % 2, k // 2, q, 4 if k % 2 == 0 else None)
                else:
                    q = A_Q0 + A_MOD_AT[k]
                    mod_slot(q % 4, 48 * i + q_round(q), k % 2, k // 2, 12 * i + q,
                             2 * i + (3 + k // 2) if k % 2 == 0 else None)

            def convolve(i, u, n, t):
                w = cols[:, bass.ds(2 * i + (C_CONV + KE * t + u), 1)]
                if t == 1:
                    dve.wait_ge(xh_used, 2 * i + (u + 1))
                    return step(dve.tensor_scalar(work[:, u, :], tmp[:, 2 + u, :], w, None, ALU.mult))
                after(n)
                to, fro = ((1, S), (0, S - 1)) if t == 0 else ((0, S - 1), (1, S))
                return step(dve.scalar_tensor_tensor(out=work[:, u, to[0]:to[1]], in0=tmp[:, 2 + u, fro[0]:fro[1]],
                                                     scalar=w, in1=work[:, u, to[0]:to[1]],
                                                     op0=ALU.mult, op1=ALU.add))

            def layer_a(i):
                first = isinstance(i, int)

                def cut(s):
                    if first:
                        cut_lo_start(s + LEAD)
                    else:
                        q = A_Q0 + A_W_AT[s]
                        cut_lo(8 * i + (s + LEAD + 1), ((s + LEAD) % 4, q % 4))

                if not first:
                    group_slot(i, 0)
                    cut(0)
                    cut(1)
                    group_slot(i, 1)
                    cut(2)
                    cut(3)
                    group_slot(i, 2)
                else:
                    group_slot(i, 0)
                    cut(3)
                    group_slot(i, 1)
                for u in range(2):
                    dve.wait_ge(cg_ready, 2 * i + (u + 1))
                    dve.wait_ge(blocks, 16 * i + (FREE + (10 if first else 6 + u + 1)))
                    dve.tensor_tensor(tmp[:, 2 + u, :], tmp[:, 2 + u, :], pp[2 + u][:, :],
                                      ALU.mult).then_inc(xh_used, 1)
                cut(4)
                n = [convolve(i, u, None, 1) for u in range(2)]
                n = [convolve(i, u, n[u], 0) for u in range(2)]
                n = [convolve(i, u, n[u], 2) for u in range(2)]
                if first:
                    group_slot(i, 2)
                group_slot(i, 3)
                cut(5)
                cut(6)
                for u in range(2):
                    after(n[u])
                    dve.wait_ge(sz_ready, 2 * i + (FREE + u + 1))
                    n[u] = step(dve.tensor_tensor(work[:, u, :], work[:, u, :], tmp[:, u, :], ALU.mult))
                cut(7)
                for u in range(2):
                    after(n[u])
                    dve.wait_ge(blocks, 16 * i + (FREE + 14 + u + 1))
                    dve.tensor_tensor(work[:, u, :], work[:, u, :], pp[2 + u][:, :], ALU.mult).then_inc(bg_used, 1)
                cut_y(i, bg_used, 2 * i + FREE)
                dve.wait_ge(acc_used, 2 * i + 6)
                step(dve.tensor_tensor(mod[:, bass.ds(4 * i + 16, 4)], p_small[:, 0:4],
                                       cols[:, bass.ds(4 * i + (C_BMOD + 16), 4)], ALU.add))

            def cut_y(i, made, base):
                n = []
                for u in range(2):
                    dve.wait_ge(made, base + (u + 1))
                    n.append(step(dve.tensor_scalar(y_hi[:, bass.ds(2 * i + u, 1), :], work[:, u, :], 1.0, None,
                                                    ALU.mult)))
                for u in range(2):
                    after(n[u])
                    dve.tensor_tensor(y_lo[:, bass.ds(2 * i + u, 1), :], work[:, u, :],
                                      f32(y_hi[:, bass.ds(2 * i + u, 1), :]), ALU.subtract).then_inc(y_cut, 1)

            layer_a(0)
            loop(1, PAIRS, 4 * 3 + 3 * 2 + 2 + 2 + 1, layer_a)

            def gate(layer, k):
                c = 3 * KD * layer + 2 * KD
                return mod[:, bass.ds(k + c, 1)] if not isinstance(k, int) else mod[:, c + k:c + k + 1]

            def update_x(layer, j):
                for u in range(2):
                    w = (W_AOUT, W_BOUT)[layer]
                    dve.wait_ge(blocks, 8 * j + (FREE + 2 * w + 6 + u + 1))
                    xa = x[:, bass.ds(2 * j + u, 1), :]
                    dve.scalar_tensor_tensor(out=xa, in0=pp[u][:, :], scalar=gate(layer, 2 * j + u), in1=xa,
                                             op0=ALU.mult, op1=ALU.add).then_inc(x_updated, 1)
                for u in range(2):
                    add_squares(layer, 2 * j + (u + 1), tmp[:, 2 + u, :], ALL)

            def update_half(layer, half):
                w = (W_AOUT, W_BOUT)[layer]
                for u in range(2):
                    if half == 0:
                        dve.wait_ge(half_done, 3 * layer + 1)
                    else:
                        dve.wait_ge(blocks, 8 * (DPAIRS - 1) + FREE + 2 * w + 6 + u + 1)
                    xa = x[:, 6 + u, halves[half]]
                    dve.scalar_tensor_tensor(out=xa, in0=pp[2 * half + u][:, 0:HALF], scalar=gate(layer, 6 + u), in1=xa,
                                             op0=ALU.mult, op1=ALU.add).then_inc(x_updated, 1)

            def add_half(layer, half):
                for u in range(2):
                    add_squares(layer, 6 + 2 * half + u + 1, work[:, 1, HALF * u:HALF * (u + 1)],
                                halves[half])

            def start_rstd(k, half):
                dve.wait_ge(stat_sum, k if k < 4 else k - 1)
                rsqrt(k, p_half[half][:, 0:2], 1.0 / D, 2)

            dve.wait_ge(ws_hi_cut, 1)
            dve.tensor_tensor(ws_lo[:, :], rs_bc[:, :], f32(ws_hi[:, :]), ALU.subtract).then_inc(ws_cut, 1)
            after(at[0])
            dve.scalar_tensor_tensor(
                out=amp[:, KD:2 * KD], in0=mod[:, 4 * KD:5 * KD], scalar=1.0,
                in1=cols[:, C_NORM + KD:C_NORM + 2 * KD], op0=ALU.add, op1=ALU.mult).then_inc(x_updated, 1)
            with dve.Fori(0, DPAIRS - 1) as j:
                for s in range(4):
                    cut_lo_late(j + W_AOUT // 4, s)
                update_x(0, j)
            n = W_AOUT // 4 + DPAIRS - 1
            cut_lo_late(n, 0)
            update_half(0, 0)
            add_half(0, 0)
            cut_lo_late(n, 1)
            start_rstd(2, 0)
            cut_lo_late(n, 2)
            diagonals(2, 2, 0)
            dve.wait_ge(rstd_bc, 2)
            half0, half1 = (p_half[half][:, 0:HALF] for half in range(2))
            scale_pair(KD, 0, half0, halves[0])
            cut_lo_late(n, 3)
            scale_pair(KD, 1, half0, halves[0])
            cut_h_pair(KD, 0, halves[0])
            update_half(0, 1)
            dve.wait_ge(h_cut, KD + 2)
            scale_pair(KD, 2, half0, halves[0])
            cut_h_pair(KD, 1, halves[0])
            cut_lo_late(W_BV // 4, 0)
            add_half(0, 1)
            dve.wait_ge(h_cut, KD + 4)
            scale_pair(KD, 3, half0, halves[0])
            cut_h_pair(KD, 2, halves[0])
            cut_h_pair(KD, 3, halves[0])
            start_rstd(3, 1)
            diagonals(3, 2, 2)
            dve.wait_ge(rstd_bc, 3)
            scale_pair(2 * KD, 0, half1, halves[1])
            scale_pair(2 * KD, 1, half1, halves[1])
            for kp in range(4):
                cut_h_pair(2 * KD, kp, halves[1])
                if kp < 2:
                    dve.wait_ge(h_cut, 2 * KD + 2 * kp + 2)
                    scale_pair(2 * KD, kp + 2, half1, halves[1])

            def v_parts(c, sts):
                n = {}
                for st in sts:
                    dve.wait_ge(v_gelu, 4 * c + (st + 1))
                    step(dve.bn_stats(bstat[:, st, bass.ds(c, 1), :], tmp[:, st, :]))
                    n[st] = step(dve.tensor_scalar(y_hi[:, bass.ds(4 * c, 4), P * st:P * (st + 1)],
                                                   tmp[:, st, :].rearrange("p (m e) -> p m e", e=P), 1.0, None,
                                                   ALU.mult))
                    if st > sts[0]:
                        v_low(c, st - 1, n)
                v_low(c, sts[-1], n)

            def v_low(c, st, n):
                after(n[st])
                dve.tensor_tensor(y_lo[:, bass.ds(4 * c, 4), P * st:P * (st + 1)],
                                  tmp[:, st, :].rearrange("p (m e) -> p m e", e=P),
                                  f32(y_hi[:, bass.ds(4 * c, 4), P * st:P * (st + 1)]),
                                  ALU.subtract).then_inc(v_cut, 1)

            def layer_b_v(c):
                for s in range(4):
                    cut_lo_late(c + W_BV // 4, s)
                v_parts(c, range(NCH))

            v_parts(0, range(2))
            for s in range(1, 4):
                cut_lo_late(W_BV // 4, s)
            v_parts(0, range(2, NCH))
            loop(1, 4, 2 * NCH, layer_b_v)

            for st in range(NCH):
                step(dve.bn_aggr(mv[:, st, :], bstat[:, st, :, :]))
            after(at[0])
            rsqrt(4, mv[:, :, 1], 1.0, NCH)
            dve.wait_ge(power_ready, 4)
            ln_rstd = small[:, 5, :]
            after(step(dve.tensor_copy(ln_rstd, small[:, 2, :])))
            dve.wait_ge(bs_in, 16)
            dve.wait_ge(sv_used, 2)

            def layer_b_uz(i):
                cut_lo_late(i + W_BUZ // 4, 0)
                dve.wait_ge(v_cut, 16 + FREE)
                dve.wait_ge(sv_done, 2 * i + FREE)
                dve.wait_ge(y_cut, 2 * i + (KE + FREE))
                vt = work[:, :, :].rearrange("p a (b e) -> p a b e", e=P)
                n, k = [], []
                for st in range(NCH):
                    src_hi, src_lo = (a[:, bass.ds(2 * i, 2), P * st:P * (st + 1)] for a in (y_hi, y_lo))
                    n.append(step(dve.scalar_tensor_tensor(out=vt[:, :, st, :], in0=f32(src_hi),
                                                           scalar=mv[:, st, 0:1], in1=f32(src_lo),
                                                           op0=ALU.subtract, op1=ALU.add)))
                for st in range(NCH):
                    after(n[st])
                    k.append(step(dve.tensor_scalar(vn_hi[:, :, P * st:P * (st + 1)], vt[:, :, st, :],
                                                    ln_rstd[:, st:st + 1], None, ALU.mult)))
                cut_lo_late(i + W_BUZ // 4, 1)
                for st in range(NCH):
                    after(k[st])
                    dve.scalar_tensor_tensor(out=vn_lo[:, :, P * st:P * (st + 1)], in0=vt[:, :, st, :],
                                             scalar=ln_rstd[:, st:st + 1],
                                             in1=f32(vn_hi[:, :, P * st:P * (st + 1)]),
                                             op0=ALU.mult, op1=ALU.subtract).then_inc(vn_cut, 1)
                n = []
                for u in range(2):
                    n.append(step(dve.scalar_tensor_tensor(
                        out=term[:, u, :], in0=rs_bc[:, bass.ds(P * i, P)],
                        scalar=cols[:, bass.ds(2 * i + (C_LNB + u), 1)], in1=bs_bc[:, bass.ds(P * i, P)],
                        op0=ALU.mult, op1=ALU.add)))
                cut_lo_late(i + W_BUZ // 4, 2)
                dve.wait_ge(vn_cut, 4 * i + 4)
                for u in range(2):
                    dve.wait_ge(sv_done, 2 * i + (FREE + u + 1))
                    after(n[u])
                    tb = term[:, u, :].unsqueeze(1).broadcast_to([P, NCH, P])
                    dve.scalar_tensor_tensor(out=work[:, u, :].rearrange("p (b e) -> p b e", e=P),
                                             in0=p_sv[u][:, :].rearrange("p (b e) -> p b e", e=P),
                                             scalar=cols[:, bass.ds(2 * i + (C_LNG + u), 1)], in1=tb,
                                             op0=ALU.mult, op1=ALU.add).then_inc(sv_used, 1)
                n = []
                for u in range(2):
                    dve.wait_ge(sv_used, 2 * i + (2 + u + 1))
                    dve.wait_ge(u_gelu, 2 * i + (FREE + u + 1))
                    n.append(step(dve.tensor_tensor(work[:, u, :], work[:, u, :], tmp[:, 2 + u, :], ALU.mult)))
                cut_lo_late(i + W_BUZ // 4, 3)
                for u in range(2):
                    after(n[u])
                    dve.wait_ge(z_silu, 2 * i + (FREE + u + 1))
                    n[u] = step(dve.tensor_tensor(work[:, u, :], work[:, u, :], tmp[:, u, :], ALU.mult))
                cut_y(i, dve_step, n[0] - 1)

            loop(0, PAIRS, 4 + 4 + 2 + 2 + 2 + 2, layer_b_uz)

            dve.sem_inc(x_updated, 1)
            with dve.Fori(0, DPAIRS - 1) as j:
                for s in range(4):
                    cut_lo_late(j + W_BOUT // 4, s)
                update_x(1, j)
            cut_lo_late(W_BOUT // 4 + DPAIRS - 1, 0)

            for half in range(2):
                update_half(1, half)
                add_half(1, half)
                start_rstd(5 + half, half)
                diagonals(5 + half, 2, 2 * half)
                dve.wait_ge(rstd_bc, 4 + half)
                for k in range(KD):
                    xa = x[:, k, halves[half]]
                    dve.scalar_tensor_tensor(out=xa, in0=xa, scalar=cols[:, C_FG + k:C_FG + k + 1],
                                             in1=p_half[half][:, 0:HALF], op0=ALU.mult,
                                             op1=ALU.mult).then_inc(out_ready, 1)


def _slot(w, row, col, n_tiles, width):
    part = w[row:row + n_tiles * P, col:col + width].reshape(n_tiles, P, width)
    return part.transpose(1, 0, 2).reshape(P, n_tiles * width)


def _stream(w_mod, a_in, a_out, b_in, b_out):
    def mod_group(g, half):
        return _slot(w_mod[g // 12], 512 * half, 256 * (g % 12), 4, 256)

    w = []
    for i in range(PAIRS):
        for col in (2 * E, 3 * E, 0, E):
            w += [_slot(a_in, 512 * half, col + 256 * i, 4, 256) for half in range(2)]
    for j in range(DPAIRS):
        w += [_slot(a_out, 512 * s, 256 * j, 4, 256) for s in range(4)]
    for c in range(4):
        w += [_slot(b_in, 256 * s, 2 * E + 512 * c, 2, 512) for s in range(4)]
    for i in range(PAIRS):
        for col in (E, 0):
            w += [_slot(b_in, 512 * half, col + 256 * i, 4, 256) for half in range(2)]
    for j in range(DPAIRS):
        w += [_slot(b_out, 512 * s, 256 * j, 4, 256) for s in range(4)]
    first = iter(np.concatenate([_slot(a_in, 256 * kp, col, 2, 256).reshape(P, 2, 256) for col in (2 * E, 3 * E)],
                                axis=2).reshape(P, SLOT) for kp in range(4))
    w[0:8] = [next(first), next(first), w[4], next(first), next(first), w[5], w[6], w[7]]

    def start_slot(kp, j):
        parts = [_slot(w_mod[0], 256 * j, col + 256 * kp, 2, 256).reshape(P, 2, 256) for col in (D, 0)]
        return np.concatenate(parts, axis=2).reshape(P, SLOT)

    def from_order(order, i, base):
        for n, what in enumerate(order):
            if not isinstance(what, str):
                yield w[base + what]
            elif what[0] == "s":
                yield start_slot(int(what[1]), order[:n].count(what))
            else:
                k = int(what[1])
                yield mod_group(8 + 2 * i + k // 2, k % 2)

    q = list(from_order(START_ORDER, 0, 0))
    for i in range(1, PAIRS):
        q += from_order(A_ORDER, i, 8 * i + LEAD)
    q += w[8 * PAIRS + LEAD:]
    return np.stack(q)


def kernel(x, c, norm_g, w_mod, b_mod, a_w_in, a_w_conv, a_w_out, b_w_in, b_ln_g, b_ln_b, b_w_s, b_b_s, b_w_out,
           final_g):
    import concourse.bacc as bacc
    from concourse.bass_utils import run_bass_kernel_spmd

    a = {k: np.asarray(v) for k, v in dict(x=x, c=c, norm_g=norm_g, w_mod=w_mod, b_mod=b_mod, a_w_in=a_w_in,
         a_w_conv=a_w_conv, a_w_out=a_w_out, b_w_in=b_w_in, b_ln_g=b_ln_g, b_ln_b=b_ln_b, b_w_s=b_w_s, b_b_s=b_b_s,
         b_w_out=b_w_out, final_g=final_g).items()}
    rows = [a["norm_g"], a["b_mod"], a["c"], a["b_ln_g"], a["b_ln_b"], a["final_g"], a["a_w_conv"][0].T]
    arrays = {
        "stream": _stream(a["w_mod"], a["a_w_in"][0], a["a_w_out"][0], a["b_w_in"][0], a["b_w_out"][0]),
        "xt": np.ascontiguousarray(a["x"][0].T.reshape(KD, P, S).transpose(1, 0, 2)),
        "cols": np.ascontiguousarray(np.concatenate([r.reshape(-1, P) for r in rows]).T),
        "wst": np.ascontiguousarray(a["b_w_s"][0].transpose(2, 0, 1).reshape(P, 8 * P)),
        "bs": np.ascontiguousarray(np.broadcast_to(a["b_b_s"][0].reshape(1, 8 * P), (P, 8 * P))),
    }
    nc = bacc.Bacc("TRN2", target_bir_lowering=False, num_devices=1)
    args = [nc.dram_tensor(f"in_{n}", v.shape, F32, kind="ExternalInput").ap() for n, v in arrays.items()]
    out = nc.dram_tensor("out_t", (P, KD, S), F32, kind="ExternalOutput").ap()
    build(nc, *args, out)
    r = run_bass_kernel_spmd(nc, [{f"in_{n}": v for n, v in arrays.items()}], core_ids=[0])
    return np.ascontiguousarray(r.results[0]["out_t"].transpose(2, 1, 0).reshape(1, S, D))
```

```python
from contextlib import ExitStack

import numpy as np

import concourse.bass as bass
from concourse import mybir

F32 = mybir.dt.float32
F32R = mybir.dt.float32r
ACT = mybir.ActivationFunctionType
ALU = mybir.AluOpType

P = 128
D = 1024
S = 512
E = 2048
KD = D // P
KE = E // P
NCH = S // P
HALF = S // 2
EPS = 1e-6

SLOT = 1024
RING = 4
N_RSQRT = 6
X_STEPS = KD + 2 + 1
SQUARES = KD + 2
SQ_STEPS = 1 + 6 + 2
SQ_START = 5
DIRECT = (3, 5)
FREE = 2
WARM = (15, 3, 12)
WARM_END = 8
LEAD = 3
PAIRS = KE // 2
DPAIRS = KD // 2

W_AOUT = 8 * PAIRS
W_BV = W_AOUT + 4 * DPAIRS
W_BUZ = W_BV + 16
W_BOUT = W_BUZ + 4 * PAIRS
W_END = W_BOUT + 4 * DPAIRS
Q_END = 4 * DPAIRS + 4 * PAIRS + W_END
Q_MINUS_W = Q_END - W_END
START_ORDER = (["s0"] * 4 + [0] + ["s1"] * 4 + [2, 1] + ["s2"] * 4 + [3] + ["s3"] * 4
               + [5, 4, "m0", 6, "m1", 7, "m2", "m3", 8, 9, 10])
S_AT = [[q for q, what in enumerate(START_ORDER) if what == f"s{kp}"] for kp in range(4)]
CUT_ORDER = [what for what in START_ORDER if not isinstance(what, str)]
Q_START = len(START_ORDER)
A_ORDER = ["m0", 0, 1, "m1", 2, 3, "m2", 4, "m3", 5, 6, 7]
A_MOD_AT = [A_ORDER.index(f"m{k}") for k in range(4)]
A_W_AT = [A_ORDER.index(k) for k in range(8)]
A_Q0 = Q_START - len(A_ORDER)

C_NORM = 0
C_BMOD = C_NORM + 2 * KD
C_C = C_BMOD + 6 * KD
C_LNG = C_C + KD
C_LNB = C_LNG + KE
C_FG = C_LNB + KE
C_CONV = C_FG + KD
N_COL = C_CONV + 3 * KE


def build(nc, stream, xt, cols_d, wst_d, bs_d, out):
    ctx = ExitStack()
    with ctx:
        def sb(name, shape, dt=F32):
            return ctx.enter_context(nc.sbuf_tensor(name, shape, dt))

        def sem(name):
            return ctx.enter_context(nc.semaphore(name))

        raw = sb("raw", [P, RING, SLOT])
        w_hi = sb("w_hi", [P, RING, SLOT], F32R)
        w_lo = sb("w_lo", [P, RING, SLOT], F32R)
        x = sb("x", [P, KD, S])
        h_hi = sb("h_hi", [P, KD, S], F32R)
        h_lo = sb("h_lo", [P, KD, S], F32R)
        y_hi = sb("y_hi", [P, KE, S], F32R)
        y_lo = sb("y_lo", [P, KE, S], F32R)
        ws = sb("ws", [P, 8, 2, P], F32R)
        vn_hi = sb("vn_hi", [P, 2, S], F32R)
        vn_lo = sb("vn_lo", [P, 2, S], F32R)
        rs_bc = sb("rs_bc", [P, 8 * P])
        bs_bc = sb("bs_bc", [P, 8 * P])
        tmp = sb("tmp", [P, 4, S])
        work = sb("work", [P, 2, S])
        ssum = sb("ssum", [P, S])
        term = sb("term", [P, 2, P])
        acc = sb("acc", [P, 2, S])
        cols = sb("cols", [P, N_COL])
        silu_c = sb("silu_c", [P, KD])
        mod = sb("mod", [P, 6 * KD])
        amp = sb("amp", [P, 2 * KD])
        variance = sb("variance", [P, NCH])
        rstd = sb("rstd", [P, NCH])
        ln_rstd = sb("ln_rstd", [P, NCH])
        bstat = sb("bstat", [P, NCH, 4, 6])
        mv = sb("mv", [P, NCH, 2])
        ident = sb("ident", [P, P])
        minus_half = sb("minus_half", [P, NCH])
        ones = sb("ones", [P, P])
        ones_r = sb("ones_r", [P, P], F32R)

        pp = [ctx.enter_context(nc.psum_tensor(f"pp{b}", [P, S], F32)) for b in range(4)]
        p_aux = ctx.enter_context(nc.psum_tensor("p_aux", [P, 4, S], F32))
        p_small, p_rstd = p_aux[:, 0, :], p_aux[:, 1, :]
        p_pair = [p_aux[:, 2 + u, :] for u in range(2)]

        landed = [sem(f"landed{j}") for j in range(RING)]
        consumed = sem("consumed")
        hi_cut = sem("hi_cut")
        blocks = sem("blocks")
        cols_in, x_in, ws_in, bs_in = sem("cols_in"), [sem(f"x_in{k}") for k in range(4)], sem("ws_in"), sem("bs_in")
        consts = sem("consts")
        sc_ready = sem("sc_ready")
        acc_used = sem("acc_used")
        ws_hi_cut, ws_cut = sem("ws_hi_cut"), sem("ws_cut")
        rs_summed = sem("rs_summed")
        sq_ready = sem("sq_ready")
        sq_odd = sem("sq_odd")
        direct_done = sem("direct_done")
        sq_added = sem("sq_added")
        stat_sum, var_ready, power_ready = sem("stat_sum"), sem("var_ready"), sem("power_ready")
        half_done = sem("half_done")
        diag_ready, rstd_bc = sem("diag_ready"), sem("rstd_bc")
        rstd_copied = sem("rstd_copied")
        amp_ready = sem("amp_ready")
        h_scaled = sem("h_scaled")
        h_made, h_hi_cut, h_cut = sem("h_made"), sem("h_hi_cut"), sem("h_cut")
        cg_ready, xh_used, sz_ready, bg_used = sem("cg_ready"), sem("xh_used"), sem("sz_ready"), sem("bg_used")
        y_cut = sem("y_cut")
        x_updated = sem("x_updated")
        v_gelu, v_cut = sem("v_gelu"), sem("v_cut")
        u_gelu = sem("u_gelu")
        vn_cut, sv_done, sv_used = sem("vn_cut"), sem("sv_done"), sem("sv_used")
        z_silu = sem("z_silu")
        out_ready, out_sent = sem("out_ready"), sem("out_sent")
        dve_step = sem("dve_step")

        def q_round(q):
            return 16 * (q // RING + 1)

        ALL = slice(0, S)
        halves = [slice(0, HALF), slice(HALF, S)]

        def x_squared(k):
            return tmp[:, k, :] if k < 4 else (rs_bc, bs_bc)[k // 2 - 2][:, S * (k % 2):S * (k % 2 + 1)]

        def last_bank(layer, half):
            return 2 * ((layer + 1 + half) % 2)

        def v_bank(st):
            return pp[(st + 2) % 4]

        p_half = [p_rstd, p_pair[0]]

        free_at_start = {"act": [sz_ready, u_gelu, z_silu], "pe": [sv_done, blocks],
                         "dve": [bg_used, y_cut, x_updated, v_cut]}

        block = ctx.enter_context(nc.Block())

        @block.sync
        def _(sp):
            sp.dma_start(cols[:, :], cols_d[:, :]).then_inc(cols_in, 16)
            for k in range(4):
                sp.dma_start(x[:, 2 * k:2 * k + 2, :], xt[:, 2 * k:2 * k + 2, :]).then_inc(x_in[k], 16)
            for q in range(RING):
                sp.dma_start(raw[:, q, :], stream[q, :, :]).then_inc(landed[q], 16)
            with sp.Fori(1, Q_END // RING) as r:
                for j in range(RING):
                    sp.wait_ge(consumed, RING * r + (j - RING + 1))
                    sp.dma_start(raw[:, j, :], stream[RING * r + j, :, :]).then_inc(landed[j], 16)
            for n in range(KD):
                half, k = n // DPAIRS, 2 * (n % DPAIRS)
                sp.wait_ge(out_ready, 2 * n + 2)
                at = slice(HALF * half, HALF * (half + 1))
                sp.dma_start(out[:, k:k + 2, at], x[:, k:k + 2, at]).then_inc(out_sent, 16)
            sp.wait_ge(out_sent, 16 * KD)

        @block.gpsimd
        def _(pool):
            pool.memset(ident[:, :], 0.0).then_inc(consts, 1)
            pool.memset(ones[:, :], 1.0).then_inc(consts, 1)
            pool.wait_ge(consts, 2)
            pool.affine_select(out=ident[:, :], in_=ident[:, :], compare_op=ALU.not_equal, fill=1.0, base=0,
                               pattern=[[-1, P]], channel_multiplier=1).then_inc(consts, 1)
            pool.memset(minus_half[:, :], -0.5).then_inc(consts, 1)
            pool.wait_ge(consts, 4)
            for n, k in enumerate((3, 5)):
                pool.wait_ge(sq_ready, k + 1)
                if n:
                    pool.wait_ge(sq_odd, n)
                pool.tensor_tensor(work[:, 0, :], work[:, 0, :] if n else x_squared(1), x_squared(k),
                                   ALU.add).then_inc(sq_odd, 1)
            for k in range(N_RSQRT):
                pool.wait_ge(var_ready, k + 1)
                pool.tensor_tensor(rstd[:, :], variance[:, :], minus_half[:, :], ALU.pow).then_inc(power_ready, 1)
                if k == 0:
                    pool.wait_ge(rstd_copied, 1)
                    for kp in range(1, DPAIRS + 2):
                        if kp > 1:
                            kt = 2 * kp - 3
                            pool.wait_ge(h_hi_cut, kt + 1)
                            pool.wait_ge(h_cut, kt)
                            pool.tensor_tensor(h_lo[:, kt, :], tmp[:, kt % 4, :], h_hi[:, kt, :].bitcast(F32),
                                               ALU.subtract).then_inc(h_cut, 1)
                        for kt in (2 * kp, 2 * kp + 1):
                            if kt < KD:
                                if kt >= 4:
                                    pool.wait_ge(h_cut, kt - 3)
                                pool.tensor_tensor(tmp[:, kt % 4, :], x[:, kt, :], work[:, 1, :],
                                                   ALU.mult).then_inc(h_scaled, 1)
                if k in (0, 2):
                    pool.wait_ge(stat_sum, k + 1)
                    pool.memset(ssum[:, :], 0.0).then_inc(sq_added, 1)

        @block.scalar
        def _(act):
            for s in free_at_start["act"]:
                act.sem_inc(s, FREE)


            def cut_hi(w, slot, land, first=False):
                act.wait_ge(landed[slot[1]], land)
                if not first:
                    act.wait_ge(blocks, 2 * w - (2 * LEAD - FREE))
                act.activation(w_hi[:, slot[0], :], raw[:, slot[1], :], ACT.Copy).then_inc(hi_cut, 1)

            def cut_hi_start(w):
                q = START_ORDER.index(w)
                cut_hi(w, (w % 4, q % 4), q_round(q), first=w < LEAD)

            def cut_hi_late(n, s):
                w = s + LEAD
                cut_hi(4 * n + w, (w % 4, w % 4), 16 * (n + Q_MINUS_W // 4 + w // 4 + 1))

            def h_tiles(layer, done, tiles, at):
                for k in tiles:
                    act.wait_ge(h_scaled, done + k + 1)
                    act.activation(tmp[:, k % 4, at], tmp[:, k % 4, at], ACT.Identity,
                                   scale=amp[:, KD * layer + k:KD * layer + k + 1],
                                   bias=mod[:, 3 * KD * layer + k:3 * KD * layer + k + 1]).then_inc(h_made, 1)
                    act.wait_ge(h_made, done + k + 1)
                    act.activation(h_hi[:, k, at], tmp[:, k % 4, at], ACT.Copy).then_inc(h_hi_cut, 1)

            act.wait_ge(cols_in, 16)
            act.activation(silu_c[:, :], cols[:, C_C:C_C + KD], ACT.Silu).then_inc(sc_ready, 1)
            for k in range(KD):
                act.wait_ge(x_in[k // 2], 16)
                act.activation(x_squared(k), x[:, k, :], ACT.Square).then_inc(sq_ready, 1)
            for kp, before, after in ((0, [0], [2]), (1, [1], []), (2, [3], [5]), (3, [4], [6])):
                if kp == 0:
                    act.wait_ge(consts, 3)
                    act.wait_ge(power_ready, 1)
                    act.wait_ge(sq_added, SQ_START)
                    for st in range(2):
                        ins = act.activation(work[:, 0, P * st:P * (st + 1)], ident[:, :], ACT.Copy,
                                             scale=rstd[:, st:st + 1])
                    ins.then_inc(diag_ready, 1)
                    cut_hi_start(0)
                    act.wait_ge(h_scaled, 2)
                    act.activation(work[:, 1, :], p_rstd[:, :], ACT.Copy).then_inc(rstd_copied, 1)
                if kp:
                    for w in before:
                        cut_hi_start(w)
                act.wait_ge(amp_ready, kp + 1)
                h_tiles(0, 0, (2 * kp, 2 * kp + 1), ALL)
                for w in after:
                    cut_hi_start(w)
            act.dma_start(rs_bc[:, :], wst_d[:, :]).then_inc(ws_in, 16)
            act.dma_start(bs_bc[:, :], bs_d[:, :]).then_inc(bs_in, 16)
            for u in range(2):
                act.wait_ge(blocks, FREE + 9)
                act.wait_ge(h_cut, KD)
                act.activation(tmp[:, 2 + u, :], pp[u][:, :], ACT.Copy).then_inc(cg_ready, 1)
            cut_hi_start(7)
            cut_hi_start(8)
            for u in range(2):
                act.wait_ge(blocks, FREE + 10 + u + 1)
                act.activation(tmp[:, u, :], p_pair[u][:, :], ACT.Silu).then_inc(sz_ready, 1)
            cut_hi_start(9)
            cut_hi_start(10)

            with act.Fori(1, PAIRS) as i:
                for s in range(8):
                    q = A_Q0 + A_W_AT[s]
                    cut_hi(8 * i + (s + LEAD), ((s + LEAD) % 4, q % 4), 48 * i + q_round(q))
                    if s == 2:
                        act.wait_ge(y_cut, 2 * i + FREE)
                        for u in range(2):
                            act.wait_ge(blocks, 16 * i + (FREE + 2 + u + 1))
                            act.activation(tmp[:, 2 + u, :], pp[u][:, :], ACT.Copy).then_inc(cg_ready, 1)
                    if s == 6:
                        for u in range(2):
                            act.wait_ge(blocks, 16 * i + (FREE + 10 + u + 1))
                            act.activation(tmp[:, u, :], pp[u][:, :], ACT.Silu).then_inc(sz_ready, 1)

            def square_x(layer, j):
                for u in range(2):
                    act.wait_ge(x_updated, 2 * j + (X_STEPS * layer + FREE + u + 2))
                    act.wait_ge(sq_added, 2 * j + (SQ_START + SQ_STEPS * layer + 1))
                    act.activation(tmp[:, 2 + u, :], x[:, bass.ds(2 * j + u, 1), :], ACT.Square).then_inc(sq_ready, 1)

            def square_half(layer, half):
                for u in range(2):
                    act.wait_ge(x_updated, X_STEPS * layer + FREE + 1 + 6 + 2 * half + u + 1)
                    if half == 1:
                        act.wait_ge(stat_sum, 2 * layer + 2)
                    act.activation(work[:, 1, HALF * u:HALF * (u + 1)], x[:, 6 + u, halves[half]],
                                   ACT.Square).then_inc(sq_ready, 1)

            act.wait_ge(ws_in, 16)
            act.activation(ws[:, :, 0, :], rs_bc[:, :].rearrange("q (h p) -> q h p", p=P),
                           ACT.Copy).then_inc(ws_hi_cut, 1)
            act.wait_ge(consts, 3)
            act.activation(ones_r[:, :], ones[:, :], ACT.Copy).then_inc(ws_hi_cut, 1)
            with act.Fori(0, DPAIRS - 1) as j:
                for s in range(4):
                    cut_hi_late(j + W_AOUT // 4, s)
                square_x(0, j)
            act.wait_ge(rs_summed, 1)
            for n in range(2):
                act.activation(rs_bc[:, n * S:(n + 1) * S], p_pair[n][:, :], ACT.Copy).then_inc(sv_used, 1)
            last = W_AOUT // 4 + DPAIRS - 1
            cut_hi_late(last, 0)
            square_half(0, 0)
            cut_hi_late(last, 1)
            cut_hi_late(last, 2)
            h_tiles(1, KD, [0, 1], halves[0])
            cut_hi_late(last, 3)
            h_tiles(1, KD, [2, 3, 4], halves[0])
            square_half(0, 1)
            h_tiles(1, KD, [5], halves[0])
            cut_hi_late(W_BV // 4, 0)
            h_tiles(1, KD, [6, 7], halves[0])
            h_tiles(1, 2 * KD, range(6), halves[1])
            cut_hi_late(W_BV // 4, 1)
            h_tiles(1, 2 * KD, [6, 7], halves[1])

            def v_gelus(c, sts, wait):
                for st in sts:
                    act.wait_ge(*wait(st))
                    act.activation(tmp[:, st, :], v_bank(st)[:, :], ACT.Gelu).then_inc(v_gelu, 1)

            act.wait_ge(h_cut, 3 * KD)
            v_gelus(0, (0, 1), lambda st: (half_done, 4))
            for s in range(2, 4):
                cut_hi_late(W_BV // 4, s)
            v_gelus(0, (2, 3), lambda st: (blocks, FREE + 2 * W_BV + 6 + st - 1))
            with act.Fori(1, 4) as c:
                for s in range(4):
                    cut_hi_late(c + W_BV // 4, s)
                act.wait_ge(v_cut, 4 * c + FREE)
                v_gelus(c, range(NCH), lambda st: (blocks, 8 * c + (FREE + 2 * W_BV + 6 + st // 2 + 1)))

            with act.Fori(0, PAIRS) as i:
                for s in range(4):
                    cut_hi_late(i + W_BUZ // 4, s)
                    if s == 2:
                        act.wait_ge(v_cut, 16 + FREE)
                        act.wait_ge(y_cut, 2 * i + (KE + FREE))
                        for u in range(2):
                            act.wait_ge(blocks, 8 * i + (FREE + 2 * W_BUZ + 2 + u + 1))
                            act.activation(tmp[:, 2 + u, :], pp[2 + u][:, :], ACT.Gelu).then_inc(u_gelu, 1)
                for u in range(2):
                    act.wait_ge(blocks, 8 * i + (FREE + 2 * W_BUZ + 6 + u + 1))
                    act.activation(tmp[:, u, :], pp[u][:, :], ACT.Silu).then_inc(z_silu, 1)

            with act.Fori(0, DPAIRS - 1) as j:
                for s in range(4):
                    cut_hi_late(j + W_BOUT // 4, s)
                square_x(1, j)
            cut_hi_late(W_BOUT // 4 + DPAIRS - 1, 0)
            square_half(1, 0)
            square_half(1, 1)

        @block.tensor
        def _(pe):
            for s in free_at_start["pe"]:
                pe.sem_inc(s, FREE)

            def unit(out, stationary, rhs_hi, rhs_lo, kts, first, last):
                for n, kt in enumerate(kts):
                    hi, lo = stationary(n)
                    pe.matmul(out, hi, rhs_hi(kt), start=first and n == 0, stop=False)
                    pe.matmul(out, hi, rhs_lo(kt), start=False, stop=False)
                    mm = pe.matmul(out, lo, rhs_hi(kt), start=False, stop=last and n == len(kts) - 1)
                return mm

            def weights(ring, u, width=256):
                return lambda n: tuple(a[:, ring, width * n + P * u:width * n + P * (u + 1)] for a in (w_hi, w_lo))

            def rows(a, at=ALL):
                return lambda kt: a[:, kt, at]

            def keep_clock(n):
                for _ in range(n):
                    pe.matmul(pp[3][:, 0:P], ones[:, :], ones[:, :], start=True, stop=True)

            def mod_columns(pairs, used, begun=False):
                pe.wait_ge(consumed, used)
                for col, parts in pairs:
                    for n, part in enumerate(parts):
                        mm = pe.matmul(p_small[:, col:col + 1], part, ones[:, 0:1], start=n == 0 and not begun,
                                       stop=n == len(parts) - 1, skip_group_check=begun)
                mm.then_inc(acc_used, 1)

            def group_columns(n, used):
                mod_columns([(2 * n + t, [acc[:, n, P * t:P * (t + 1)]]) for t in range(2)], used)

            def half_sums(layer, half):
                pe.wait_ge(sq_added, SQ_START + SQ_STEPS * layer + 1 + 6 + half + 1)
                for st in range(2):
                    pe.matmul(p_half[half][:, st:st + 1], ssum[:, HALF * half + P * st:HALF * half + P * (st + 1)],
                              ones[:, 0:1], start=st == 0, stop=False, skip_group_check=True)
                pe.wait_ge(sq_ready, KD + SQUARES * layer + 6 + 2 * half + 2)
                for st in range(2):
                    mm = pe.matmul(p_half[half][:, st:st + 1], work[:, 1, HALF + P * st:HALF + P * (st + 1)],
                                   ones[:, 0:1], start=False, stop=True, skip_group_check=True)
                mm.then_inc(stat_sum, 1)

            def broadcast(out, n, at):
                pe.wait_ge(diag_ready, n)
                pe.matmul(out, ones[:, :], work[:, 0, at], start=True, stop=True).then_inc(rstd_bc, 1)

            def start_columns(kp):
                mod_columns([(4 * kp + t, [acc[:, kp % 2, P * t:P * (t + 1)]]) for t in range(4)], S_AT[kp][3] + 1,
                            begun=kp == 0)

            def direct_columns():
                for n, kt in enumerate(DIRECT):
                    q = S_AT[0][kt // 2]
                    pe.wait_ge(landed[q % 4], q_round(q))
                    for t in range(4):
                        at = S * (kt % 2) + P * t
                        mm = pe.matmul(p_small[:, t:t + 1], raw[:, q % 4, at:at + P], silu_c[:, kt:kt + 1],
                                       start=n == 0 and t == 0, stop=False, skip_group_check=True)
                    mm.then_inc(direct_done, 1)

            pe.wait_ge(consts, 3)
            pe.wait_ge(sq_ready, 3)
            keep_clock(WARM[0])
            pe.wait_ge(sq_added, SQ_START)
            for st in range(NCH):
                mm = pe.matmul(p_rstd[:, st:st + 1], ssum[:, P * st:P * (st + 1)], ones[:, 0:1], start=True, stop=True)
            mm.then_inc(stat_sum, 1)
            pe.wait_ge(sc_ready, 1)
            direct_columns()
            keep_clock(WARM[1])
            broadcast(p_rstd[:, :], 2, ALL)
            start_columns(0)
            keep_clock(WARM[2])
            for kp in range(4):
                w = (0, 1, 3, 4)[kp]
                pe.wait_ge(consumed, START_ORDER.index(w) + 1)
                def part(b, u, n, stationary, moving, start, stop):
                    at = slice(S * n + P * (2 * b + u), S * n + P * (2 * b + u + 1))
                    return pe.matmul(pp[2 * b + u][:, :], stationary[:, w % 4, at], moving[:, 2 * kp + n, :],
                                     start=start, stop=stop)

                for n in range(2):
                    k = 2 * kp + n
                    if k == 0:
                        pe.wait_ge(h_hi_cut, 1)
                        for s in (w_hi, w_lo):
                            for b in range(2):
                                for u in range(2):
                                    part(b, u, n, s, h_hi, s is w_hi, False)
                    pe.wait_ge(h_cut, k + 1)
                    for b in range(2):
                        for u in range(2):
                            if k:
                                part(b, u, n, w_hi, h_hi, False, False)
                                part(b, u, n, w_lo, h_hi, False, False)
                            mm = part(b, u, n, w_hi, h_lo, False, k == KD - 1)
                        if n == 1:
                            mm.then_inc(blocks, 1)
                if kp < 3:
                    start_columns(kp + 1)
                w = (2, 5)[kp // 2]
                pe.wait_ge(consumed, START_ORDER.index(w) + 1)
                for u in range(2):
                    for n in range(2):
                        k = 2 * kp + n
                        at = slice(256 * (k % 4) + P * u, 256 * (k % 4) + P * (u + 1))
                        mm = unit(p_pair[u][:, :], lambda _: (w_hi[:, w % 4, at], w_lo[:, w % 4, at]),
                                  rows(h_hi), rows(h_lo), (k,), k == 0, k == KD - 1)
                    if kp % 2:
                        mm.then_inc(blocks, 1)
            pe.wait_ge(xh_used, 2)
            for w in (6, 7):
                pe.wait_ge(consumed, START_ORDER.index(w) + 1)
                for u in range(2):
                    unit(pp[2 + u][:, :], weights(w % 4, u), rows(h_hi), rows(h_lo), range(4 * (w - 6), 4 * (w - 5)),
                         w == 6, w == 7).then_inc(blocks, 1)
            for n in range(2):
                group_columns(n, START_ORDER.index(f"m{2 * n + 1}") + 1)
            pe.wait_ge(sz_ready, 2 + FREE)

            with pe.Fori(1, PAIRS) as i:
                for s in range(8):
                    q = A_Q0 - 12 + A_W_AT[s + 8 - LEAD] if s < LEAD else A_Q0 + A_W_AT[s - LEAD]
                    pe.wait_ge(consumed, 12 * i + (q + 1))
                    if s == 0:
                        pe.wait_ge(sz_ready, 2 * i + FREE)
                    if s == 2:
                        pe.wait_ge(bg_used, 2 * i + FREE)
                    if s == 4:
                        pe.wait_ge(cg_ready, 2 * i + 2)
                    if s == 6:
                        pe.wait_ge(xh_used, 2 * i + 2)
                    for u in range(2):
                        unit(pp[2 * (s // 2 % 2) + u][:, :], weights(s % 4, u), rows(h_hi), rows(h_lo),
                             range(4 * (s % 2), 4 * (s % 2) + 4), s % 2 == 0, s % 2 == 1).then_inc(blocks, 1)
                    if s in (4, 6):
                        n = s // 2 - 2
                        group_columns(n, 12 * i + (A_Q0 + A_MOD_AT[2 * n + 1] + 1))

            def out_slot(layer, w0, j, s):
                pe.wait_ge(consumed, 4 * j + (w0 + s + Q_MINUS_W + 1))
                pe.wait_ge(y_cut, KE * layer + 4 * (s + 1) + FREE)

            def out_product(layer, w0, j):
                for s in range(4):
                    out_slot(layer, w0, j, s)
                    for u in range(2):
                        if s == 0:
                            pe.wait_ge(x_updated, 2 * j + (X_STEPS * layer + FREE + u))
                        unit(pp[2 * layer + u][:, :], weights(s, u), rows(y_hi), rows(y_lo),
                             range(4 * s, 4 * s + 4), s == 0, s == 3).then_inc(blocks, 1)

            def last_out_product(layer, w0):
                for half in range(2):
                    for s in range(4):
                        out_slot(layer, w0, DPAIRS - 1, s)
                        for u in range(2):
                            if s == 0 and half == 1:
                                pe.wait_ge(x_updated, X_STEPS * layer + FREE + 6 + u)
                            mm = unit(pp[last_bank(layer, half) + u][:, 0:HALF], weights(s, u), rows(y_hi, halves[half]),
                                      rows(y_lo, halves[half]), range(4 * s, 4 * s + 4), s == 0, s == 3)
                            if half == 1:
                                mm.then_inc(blocks, 1)
                            elif s == 3:
                                mm.then_inc(half_done, 1)
                            if half == 1 and s == 0 and u == 1:
                                half_sums(layer, 0)
                            if half == 1 and s == 1 and u == 1:
                                broadcast(p_half[0][:, 0:HALF], 2 * layer + 3, slice(0, HALF))

            pe.wait_ge(sz_ready, KE + FREE)
            with pe.Fori(0, DPAIRS - 1) as j:
                out_product(0, W_AOUT, j)
            pe.wait_ge(ws_cut, 1)
            pe.wait_ge(ws_hi_cut, 2)
            for n in range(2):
                for part in range(2):
                    mm = pe.matmul(p_pair[n].rearrange("q (h p) -> q h p", p=P), ones_r[:, :],
                                   ws[:, 4 * n:4 * n + 4, part, :], start=part == 0, stop=part == 1)
            mm.then_inc(rs_summed, 1)
            pe.wait_ge(bg_used, KE + FREE)
            last_out_product(0, W_AOUT)

            def v_tile(st, s, n):
                kt = 2 * s + n
                left_hi, left_lo = (a[:, kt, P * st:P * (st + 1)] for a in (h_hi, h_lo))
                right_hi, right_lo = (a[:, s, S * n:S * (n + 1)] for a in (w_hi, w_lo))
                pe.matmul(v_bank(st)[:, :], left_hi, right_hi, start=kt == 0, stop=False)
                pe.matmul(v_bank(st)[:, :], left_hi, right_lo, start=False, stop=False)
                return pe.matmul(v_bank(st)[:, :], left_lo, right_hi, start=False, stop=kt == KD - 1)

            for half in range(2):
                if half == 0:
                    pe.wait_ge(x_updated, X_STEPS + FREE - 2)
                else:
                    pe.wait_ge(x_updated, X_STEPS + FREE)
                for s in range(4):
                    pe.wait_ge(consumed, W_BV + s + Q_MINUS_W + 1)
                    for n in range(2):
                        pe.wait_ge(h_cut, KD * (1 + half) + 2 * s + n + 1)
                        for st in (2 * half, 2 * half + 1):
                            mm = v_tile(st, s, n)
                            if half == 1 and n == 1:
                                mm.then_inc(blocks, 1)
                    if half == 0 and s == 1:
                        pe.wait_ge(sv_used, 2)
                        half_sums(0, 1)
                    if half == 0 and s == 2:
                        broadcast(p_half[1][:, 0:HALF], 4, slice(HALF, S))
                if half == 0:
                    mm.then_inc(half_done, 2)
            with pe.Fori(1, 4) as c:
                for s in range(4):
                    pe.wait_ge(consumed, 4 * c + (W_BV + s + Q_MINUS_W + 1))
                    for st in range(NCH):
                        if s == 0:
                            pe.wait_ge(v_gelu, 4 * c + (st - 3))
                        for n in range(2):
                            mm = v_tile(st, s, n)
                        if st % 2:
                            mm.then_inc(blocks, 1)

            pe.wait_ge(v_gelu, 14)
            with pe.Fori(0, PAIRS) as i:
                for s in range(4):
                    pe.wait_ge(consumed, 4 * i + (W_BUZ + s + Q_MINUS_W + 1))
                    if s == 0:
                        pe.wait_ge(u_gelu, 2 * i + FREE)
                    if s == 2:
                        pe.wait_ge(v_gelu, 16)
                        pe.wait_ge(z_silu, 2 * i + FREE)
                    if s == 3:
                        pe.wait_ge(sv_used, 2 * i + 2)
                        for u in range(2):
                            for n in range(NCH):
                                pe.wait_ge(vn_cut, 4 * i + (n + 1))
                                at = slice(P * n, P * (n + 1))
                                o = p_aux[:, 2 * u + n // 2, 256 * (n % 2):256 * (n % 2 + 1)]
                                pe.matmul(o.rearrange("p (a e) -> p a e", a=2), vn_hi[:, u, at],
                                          ws[:, bass.ds(i, 1), :, :].rearrange("q h a p -> q (h a) p"),
                                          start=True, stop=False)
                                mm = pe.matmul(o[:, 0:P], vn_lo[:, u, at],
                                               ws[:, bass.ds(i, 1), 0, :].rearrange("q h p -> q (h p)"),
                                               start=False, stop=True)
                            mm.then_inc(sv_done, 1)
                    for u in range(2):
                        unit(pp[2 * (1 - s // 2) + u][:, :], weights(s, u), rows(h_hi), rows(h_lo),
                             range(4 * (s % 2), 4 * (s % 2) + 4), s % 2 == 0, s % 2 == 1).then_inc(blocks, 1)

            pe.wait_ge(u_gelu, KE + FREE)
            with pe.Fori(0, DPAIRS - 1) as j:
                out_product(1, W_BOUT, j)
            pe.wait_ge(z_silu, KE + FREE)
            pe.wait_ge(sv_used, 2 + KE)
            last_out_product(1, W_BOUT)
            half_sums(1, 1)
            keep_clock(WARM_END)
            broadcast(p_half[1][:, 0:HALF], 6, slice(HALF, S))

        @block.vector
        def _(dve):
            for s in free_at_start["dve"]:
                dve.sem_inc(s, FREE)
            dve.sem_inc(x_updated, 1)
            at = [0]

            def step(ins):
                ins.then_inc(dve_step, 1)
                at[0] = at[0] + 1
                return at[0]

            def after(n):
                dve.wait_ge(dve_step, n)

            def loop(start, end, steps, body):
                base = at[0]
                with dve.Fori(start, end) as i:
                    at[0] = i * steps + (base - start * steps)
                    body(i)
                at[0] = base + (end - start) * steps

            def f32(ap):
                return ap.bitcast(F32)

            def cut_lo(n, slot):
                dve.wait_ge(hi_cut, n)
                dve.tensor_tensor(w_lo[:, slot[0], :], raw[:, slot[1], :], f32(w_hi[:, slot[0], :]),
                                  ALU.subtract).then_inc(consumed, 1)

            def cut_lo_start(w):
                cut_lo(CUT_ORDER.index(w) + 1, (w % 4, START_ORDER.index(w) % 4))

            def cut_lo_late(n, s):
                w = s + LEAD
                cut_lo(4 * n + (w + 1), (w % 4, w % 4))

            start_at = [None, 0]

            def start_tile(kp, kt):
                q, n = S_AT[kp][kt // 2], kt % 2
                a, w = acc[:, kp % 2, :], raw[:, q % 4, S * n:S * (n + 1)]
                if n == 0:
                    dve.wait_ge(landed[q % 4], q_round(q))
                if kt:
                    dve.wait_ge(*start_at)
                    ins = dve.scalar_tensor_tensor(out=a, in0=w, scalar=silu_c[:, kt:kt + 1], in1=a,
                                                   op0=ALU.mult, op1=ALU.add)
                else:
                    ins = dve.tensor_scalar(a, w, silu_c[:, kt:kt + 1], None, ALU.mult)
                if n == 0:
                    start_at[:] = dve_step, step(ins)
                else:
                    ins.then_inc(consumed, 1)
                    start_at[:] = consumed, q + 1

            def release(n):
                dve.wait_ge(direct_done, n + 1)
                dve.sem_inc(consumed, 1)

            def start_tiles(kp, *kts):
                for kt in kts:
                    start_tile(kp, kt)

            def mod_slot(rq, land, half, buf, used, wait_acc=None):
                dve.wait_ge(landed[rq], land)
                if wait_acc is not None:
                    dve.wait_ge(acc_used, wait_acc)
                if half:
                    dve.wait_ge(consumed, used)
                for n in range(4):
                    kt = 4 * half + n
                    w = raw[:, rq, 256 * n:256 * (n + 1)]
                    a = acc[:, buf, 0:256]
                    if kt == 0:
                        ins = dve.tensor_scalar(a, w, silu_c[:, kt:kt + 1], None, ALU.mult)
                    else:
                        if n:
                            after(at[0])
                        ins = dve.scalar_tensor_tensor(out=a, in0=w, scalar=silu_c[:, kt:kt + 1], in1=a,
                                                       op0=ALU.mult, op1=ALU.add)
                    if n < 3:
                        step(ins)
                    else:
                        ins.then_inc(consumed, 1)

            def add_squares(layer, ready, n, src, where):
                dve.wait_ge(sq_ready, ready + (KD + SQUARES * layer))
                dve.wait_ge(sq_added, n + (SQ_START + SQ_STEPS * layer))
                dve.tensor_tensor(ssum[:, where], ssum[:, where], src, ALU.add).then_inc(sq_added, 1)

            def rsqrt(k, src, scale, n):
                dve.tensor_scalar(variance[:, 0:n], src, scale, EPS, ALU.mult, ALU.add).then_inc(var_ready, 1)

            def diagonals(k, n, first):
                dve.wait_ge(power_ready, k)
                for st in range(n):
                    ins = dve.tensor_scalar(work[:, 0, P * (first + st):P * (first + st + 1)], ident[:, :],
                                            rstd[:, st:st + 1], None, ALU.mult)
                    if st < n - 1:
                        step(ins)
                ins.then_inc(diag_ready, 1)

            def scale_pair(kp, scale, where):
                for k in (2 * kp, 2 * kp + 1):
                    dve.tensor_tensor(tmp[:, k % 4, where], x[:, k, where], scale, ALU.mult).then_inc(h_scaled, 1)

            def cut_h_pair(done, kp, where):
                for k in (2 * kp, 2 * kp + 1):
                    cut_h_tile(done, k, where)

            def cut_h_tile(done, k, where):
                dve.wait_ge(h_hi_cut, done + k + 1)
                dve.tensor_tensor(h_lo[:, k, where], tmp[:, k % 4, where], f32(h_hi[:, k, where]),
                                  ALU.subtract).then_inc(h_cut, 1)

            for n, k in enumerate((2, 4, 6, 7)):
                dve.wait_ge(sq_ready, k + 1)
                if n:
                    dve.wait_ge(sq_added, n)
                dve.tensor_tensor(ssum[:, :], ssum[:, :] if n else x_squared(0), x_squared(k),
                                  ALU.add).then_inc(sq_added, 1)
            dve.wait_ge(sc_ready, 1)
            start_tiles(0, 0)
            dve.wait_ge(sq_odd, 2)
            dve.wait_ge(sq_added, 4)
            dve.tensor_tensor(ssum[:, :], ssum[:, :], work[:, 0, :], ALU.add).then_inc(sq_added, 1)
            start_tiles(0, 1)
            dve.wait_ge(stat_sum, 1)
            rsqrt(1, p_rstd[:, 0:NCH], 1.0 / D, NCH)
            start_tiles(0, 2, 4)
            dve.wait_ge(power_ready, 1)
            for st in range(2, 4):
                ins = dve.tensor_scalar(work[:, 0, P * st:P * (st + 1)], ident[:, :], rstd[:, st:st + 1], None,
                                        ALU.mult)
            ins.then_inc(diag_ready, 1)
            start_tiles(0, 6)
            for n in range(len(DIRECT)):
                release(n)
            start_tiles(0, 7)
            dve.wait_ge(rstd_bc, 1)
            scale_pair(0, p_rstd[:, :], ALL)
            for kp in range(4):
                if kp == 2:
                    cut_lo_start(3)
                dve.wait_ge(acc_used, kp + 1)
                k = 2 * kp
                n = step(dve.scalar_tensor_tensor(out=amp[:, k:k + 2], in0=p_small[:, 4 * kp:4 * kp + 2], scalar=1.0,
                                                  in1=cols[:, C_BMOD + KD + k:C_BMOD + KD + k + 2],
                                                  op0=ALU.add, op1=ALU.add))
                m = step(dve.tensor_tensor(mod[:, k:k + 2], p_small[:, 4 * kp + 2:4 * kp + 4],
                                           cols[:, C_BMOD + k:C_BMOD + k + 2], ALU.add))
                after(m)
                dve.tensor_tensor(amp[:, k:k + 2], amp[:, k:k + 2], cols[:, C_NORM + k:C_NORM + k + 2],
                                  ALU.mult).then_inc(amp_ready, 1)
                if kp != 2:
                    cut_lo_start((0, 1, 3, 4)[kp])
                if kp < 3:
                    start_tiles(kp + 1, *((0, 1) if kp in (0, 2) else (0,)))
                cut_h_tile(0, 2 * kp, ALL)
                if kp < 3:
                    start_tiles(kp + 1, *((2, 3) if kp in (0, 2) else (1, 2, 3)))
                if kp < 3:
                    start_tiles(kp + 1, 4, 5, 6, 7)
                if kp % 2 == 0:
                    cut_lo_start((2, 5)[kp // 2])

            def group_slot(i, k):
                if isinstance(i, int):
                    q = START_ORDER.index(f"m{k}")
                    mod_slot(q % 4, q_round(q), k % 2, k // 2, q, 4 if k % 2 == 0 else None)
                else:
                    q = A_Q0 + A_MOD_AT[k]
                    mod_slot(q % 4, 48 * i + q_round(q), k % 2, k // 2, 12 * i + q,
                             2 * i + (3 + k // 2) if k % 2 == 0 else None)

            def convolve(i, u, n, t):
                w = cols[:, bass.ds(2 * i + (C_CONV + KE * t + u), 1)]
                if t == 1:
                    dve.wait_ge(xh_used, 2 * i + (u + 1))
                    return step(dve.tensor_scalar(work[:, u, :], tmp[:, 2 + u, :], w, None, ALU.mult))
                after(n)
                to, fro = ((1, S), (0, S - 1)) if t == 0 else ((0, S - 1), (1, S))
                return step(dve.scalar_tensor_tensor(out=work[:, u, to[0]:to[1]], in0=tmp[:, 2 + u, fro[0]:fro[1]],
                                                     scalar=w, in1=work[:, u, to[0]:to[1]],
                                                     op0=ALU.mult, op1=ALU.add))

            def layer_a(i):
                first = isinstance(i, int)

                def cut(s):
                    if first:
                        cut_lo_start(s + LEAD)
                    else:
                        q = A_Q0 + A_W_AT[s]
                        cut_lo(8 * i + (s + LEAD + 1), ((s + LEAD) % 4, q % 4))

                if not first:
                    group_slot(i, 0)
                    cut(0)
                    cut(1)
                    group_slot(i, 1)
                    cut(2)
                    cut(3)
                    group_slot(i, 2)
                else:
                    group_slot(i, 0)
                    cut(3)
                    group_slot(i, 1)
                for u in range(2):
                    dve.wait_ge(cg_ready, 2 * i + (u + 1))
                    dve.wait_ge(blocks, 16 * i + (FREE + (10 if first else 6 + u + 1)))
                    dve.tensor_tensor(tmp[:, 2 + u, :], tmp[:, 2 + u, :], pp[2 + u][:, :],
                                      ALU.mult).then_inc(xh_used, 1)
                cut(4)
                n = [convolve(i, u, None, 1) for u in range(2)]
                n = [convolve(i, u, n[u], 0) for u in range(2)]
                n = [convolve(i, u, n[u], 2) for u in range(2)]
                if first:
                    group_slot(i, 2)
                group_slot(i, 3)
                cut(5)
                cut(6)
                for u in range(2):
                    after(n[u])
                    dve.wait_ge(sz_ready, 2 * i + (FREE + u + 1))
                    n[u] = step(dve.tensor_tensor(work[:, u, :], work[:, u, :], tmp[:, u, :], ALU.mult))
                cut(7)
                for u in range(2):
                    after(n[u])
                    dve.wait_ge(blocks, 16 * i + (FREE + 14 + u + 1))
                    dve.tensor_tensor(work[:, u, :], work[:, u, :], pp[2 + u][:, :], ALU.mult).then_inc(bg_used, 1)
                cut_y(i, bg_used, 2 * i + FREE)
                dve.wait_ge(acc_used, 2 * i + 6)
                step(dve.tensor_tensor(mod[:, bass.ds(4 * i + 16, 4)], p_small[:, 0:4],
                                       cols[:, bass.ds(4 * i + (C_BMOD + 16), 4)], ALU.add))

            def cut_y(i, made, base):
                n = []
                for u in range(2):
                    dve.wait_ge(made, base + (u + 1))
                    n.append(step(dve.tensor_scalar(y_hi[:, bass.ds(2 * i + u, 1), :], work[:, u, :], 1.0, None,
                                                    ALU.mult)))
                for u in range(2):
                    after(n[u])
                    dve.tensor_tensor(y_lo[:, bass.ds(2 * i + u, 1), :], work[:, u, :],
                                      f32(y_hi[:, bass.ds(2 * i + u, 1), :]), ALU.subtract).then_inc(y_cut, 1)

            layer_a(0)
            loop(1, PAIRS, 4 * 3 + 3 * 2 + 2 + 2 + 1, layer_a)

            def gate(layer, k):
                c = 3 * KD * layer + 2 * KD
                return mod[:, bass.ds(k + c, 1)] if not isinstance(k, int) else mod[:, c + k:c + k + 1]

            def update_x(layer, j):
                for u in range(2):
                    w = (W_AOUT, W_BOUT)[layer]
                    dve.wait_ge(blocks, 8 * j + (FREE + 2 * w + 6 + u + 1))
                    xa = x[:, bass.ds(2 * j + u, 1), :]
                    dve.scalar_tensor_tensor(out=xa, in0=pp[2 * layer + u][:, :], scalar=gate(layer, 2 * j + u), in1=xa,
                                             op0=ALU.mult, op1=ALU.add).then_inc(x_updated, 1)
                for u in range(2):
                    add_squares(layer, 2 * j + (u + 1), 2 * j + (u + 1), tmp[:, 2 + u, :], ALL)

            def update_half(layer, half):
                w = (W_AOUT, W_BOUT)[layer]
                for u in range(2):
                    if half == 0:
                        dve.wait_ge(half_done, 4 * layer + u + 1)
                    else:
                        dve.wait_ge(blocks, 8 * (DPAIRS - 1) + FREE + 2 * w + 6 + u + 1)
                    xa = x[:, 6 + u, halves[half]]
                    dve.scalar_tensor_tensor(out=xa, in0=pp[last_bank(layer, half) + u][:, 0:HALF],
                                             scalar=gate(layer, 6 + u), in1=xa,
                                             op0=ALU.mult, op1=ALU.add).then_inc(x_updated, 1)
                    if u == 0 and layer == 1:
                        add_half(layer, half)

            def add_half(layer, half):
                add_squares(layer, 6 + 2 * half + 1, 6 + half + 1, work[:, 1, 0:HALF], halves[half])

            def start_rstd(k, half):
                dve.wait_ge(stat_sum, k if k < 4 else k - 1)
                rsqrt(k, p_half[half][:, 0:2], 1.0 / D, 2)

            dve.wait_ge(ws_hi_cut, 1)
            dve.tensor_tensor(ws[:, :, 1, :], rs_bc[:, :].rearrange("q (h p) -> q h p", p=P), f32(ws[:, :, 0, :]),
                              ALU.subtract).then_inc(ws_cut, 1)
            after(at[0])
            dve.scalar_tensor_tensor(
                out=amp[:, KD:2 * KD], in0=mod[:, 4 * KD:5 * KD], scalar=1.0,
                in1=cols[:, C_NORM + KD:C_NORM + 2 * KD], op0=ALU.add, op1=ALU.mult)
            with dve.Fori(0, DPAIRS - 1) as j:
                for s in range(4):
                    cut_lo_late(j + W_AOUT // 4, s)
                update_x(0, j)
            n = W_AOUT // 4 + DPAIRS - 1
            cut_lo_late(n, 0)
            update_half(0, 0)
            add_half(0, 0)
            start_rstd(2, 0)
            cut_lo_late(n, 1)
            diagonals(2, 2, 0)
            cut_lo_late(n, 2)
            dve.wait_ge(rstd_bc, 2)
            half0, half1 = (p_half[half][:, 0:HALF] for half in range(2))
            scale_pair(0, half0, halves[0])
            scale_pair(1, half0, halves[0])
            cut_h_pair(KD, 0, halves[0])
            dve.wait_ge(h_cut, KD + 2)
            scale_pair(2, half0, halves[0])
            cut_lo_late(n, 3)
            cut_h_pair(KD, 1, halves[0])
            update_half(0, 1)
            dve.wait_ge(h_cut, KD + 4)
            scale_pair(3, half0, halves[0])
            add_half(0, 1)
            cut_h_pair(KD, 2, halves[0])
            start_rstd(3, 1)
            cut_lo_late(W_BV // 4, 0)
            diagonals(3, 2, 2)
            cut_h_pair(KD, 3, halves[0])
            dve.wait_ge(rstd_bc, 3)
            scale_pair(0, half1, halves[1])
            scale_pair(1, half1, halves[1])
            for kp in range(4):
                cut_h_pair(2 * KD, kp, halves[1])
                if kp < 2:
                    dve.wait_ge(h_cut, 2 * KD + 2 * kp + 2)
                    scale_pair(kp + 2, half1, halves[1])
                if kp == 2:
                    cut_lo_late(W_BV // 4, 1)

            def v_parts(c, sts):
                n = {}
                for st in sts:
                    dve.wait_ge(v_gelu, 4 * c + (st + 1))
                    step(dve.bn_stats(bstat[:, st, bass.ds(c, 1), :], tmp[:, st, :]))
                    n[st] = step(dve.tensor_scalar(y_hi[:, bass.ds(4 * c, 4), P * st:P * (st + 1)],
                                                   tmp[:, st, :].rearrange("p (m e) -> p m e", e=P), 1.0, None,
                                                   ALU.mult))
                    if st > sts[0]:
                        v_low(c, st - 1, n)
                v_low(c, sts[-1], n)

            def v_low(c, st, n):
                after(n[st])
                dve.tensor_tensor(y_lo[:, bass.ds(4 * c, 4), P * st:P * (st + 1)],
                                  tmp[:, st, :].rearrange("p (m e) -> p m e", e=P),
                                  f32(y_hi[:, bass.ds(4 * c, 4), P * st:P * (st + 1)]),
                                  ALU.subtract).then_inc(v_cut, 1)

            def layer_b_v(c):
                for s in range(4):
                    cut_lo_late(c + W_BV // 4, s)
                v_parts(c, range(NCH))

            v_parts(0, range(2))
            for s in range(2, 4):
                cut_lo_late(W_BV // 4, s)
            v_parts(0, range(2, NCH))
            loop(1, 4, 2 * NCH, layer_b_v)

            for st in range(NCH):
                step(dve.bn_aggr(mv[:, st, :], bstat[:, st, :, :]))
            after(at[0])
            rsqrt(4, mv[:, :, 1], 1.0, NCH)
            dve.wait_ge(power_ready, 4)
            after(step(dve.tensor_copy(ln_rstd[:, :], rstd[:, :])))
            dve.wait_ge(bs_in, 16)
            dve.wait_ge(sv_used, 2)

            def layer_b_uz(i):
                cut_lo_late(i + W_BUZ // 4, 0)
                dve.wait_ge(v_cut, 16 + FREE)
                dve.wait_ge(sv_done, 2 * i + FREE)
                dve.wait_ge(y_cut, 2 * i + (KE + FREE))
                vt = work[:, :, :].rearrange("p a (b e) -> p a b e", e=P)
                n, k = [], []
                for st in range(NCH):
                    src_hi, src_lo = (a[:, bass.ds(2 * i, 2), P * st:P * (st + 1)] for a in (y_hi, y_lo))
                    n.append(step(dve.scalar_tensor_tensor(out=vt[:, :, st, :], in0=f32(src_hi),
                                                           scalar=mv[:, st, 0:1], in1=f32(src_lo),
                                                           op0=ALU.subtract, op1=ALU.add)))
                for st in range(NCH):
                    after(n[st])
                    k.append(step(dve.tensor_scalar(vn_hi[:, :, P * st:P * (st + 1)], vt[:, :, st, :],
                                                    ln_rstd[:, st:st + 1], None, ALU.mult)))
                cut_lo_late(i + W_BUZ // 4, 1)
                for st in range(NCH):
                    after(k[st])
                    dve.scalar_tensor_tensor(out=vn_lo[:, :, P * st:P * (st + 1)], in0=vt[:, :, st, :],
                                             scalar=ln_rstd[:, st:st + 1],
                                             in1=f32(vn_hi[:, :, P * st:P * (st + 1)]),
                                             op0=ALU.mult, op1=ALU.subtract).then_inc(vn_cut, 1)
                n = []
                for u in range(2):
                    n.append(step(dve.scalar_tensor_tensor(
                        out=term[:, u, :], in0=rs_bc[:, bass.ds(P * i, P)],
                        scalar=cols[:, bass.ds(2 * i + (C_LNB + u), 1)], in1=bs_bc[:, bass.ds(P * i, P)],
                        op0=ALU.mult, op1=ALU.add)))
                cut_lo_late(i + W_BUZ // 4, 2)
                dve.wait_ge(vn_cut, 4 * i + 4)
                mixed = [p_aux[:, 2 * u:2 * u + 2, :].rearrange("p b (n a e) -> p (b n) a e", a=2, e=P) for u in range(2)]
                gain = [cols[:, bass.ds(2 * i + (C_LNG + u), 1)] for u in range(2)]
                out = [work[:, u, :].rearrange("p (b e) -> p b e", e=P) for u in range(2)]
                for u in range(2):
                    dve.wait_ge(sv_done, 2 * i + (FREE + u + 1))
                    after(n[u])
                    tb = term[:, u, :].unsqueeze(1).broadcast_to([P, NCH, P])
                    n[u] = step(dve.scalar_tensor_tensor(out=out[u], in0=mixed[u][:, :, 0, :], scalar=gain[u], in1=tb,
                                                         op0=ALU.mult, op1=ALU.add))
                for u in range(2):
                    after(n[u])
                    dve.scalar_tensor_tensor(out=out[u], in0=mixed[u][:, :, 1, :], scalar=gain[u], in1=out[u],
                                             op0=ALU.mult, op1=ALU.add).then_inc(sv_used, 1)
                n = []
                for u in range(2):
                    dve.wait_ge(sv_used, 2 * i + (2 + u + 1))
                    dve.wait_ge(u_gelu, 2 * i + (FREE + u + 1))
                    n.append(step(dve.tensor_tensor(work[:, u, :], work[:, u, :], tmp[:, 2 + u, :], ALU.mult)))
                cut_lo_late(i + W_BUZ // 4, 3)
                for u in range(2):
                    after(n[u])
                    dve.wait_ge(z_silu, 2 * i + (FREE + u + 1))
                    n[u] = step(dve.tensor_tensor(work[:, u, :], work[:, u, :], tmp[:, u, :], ALU.mult))
                cut_y(i, dve_step, n[0] - 1)

            loop(0, PAIRS, 4 + 4 + 2 + 2 + 2 + 2 + 2, layer_b_uz)

            dve.sem_inc(x_updated, 1)
            with dve.Fori(0, DPAIRS - 1) as j:
                for s in range(4):
                    cut_lo_late(j + W_BOUT // 4, s)
                update_x(1, j)
            cut_lo_late(W_BOUT // 4 + DPAIRS - 1, 0)

            for half in range(2):
                update_half(1, half)
                start_rstd(5 + half, half)
                diagonals(5 + half, 2, 2 * half)
                dve.wait_ge(rstd_bc, 4 + half)
                for k in range(KD):
                    xa = x[:, k, halves[half]]
                    dve.scalar_tensor_tensor(out=xa, in0=xa, scalar=cols[:, C_FG + k:C_FG + k + 1],
                                             in1=p_half[half][:, 0:HALF], op0=ALU.mult,
                                             op1=ALU.mult).then_inc(out_ready, 1)


def _slot(w, row, col, n_tiles, width):
    part = w[row:row + n_tiles * P, col:col + width].reshape(n_tiles, P, width)
    return part.transpose(1, 0, 2).reshape(P, n_tiles * width)


def _stream(w_mod, a_in, a_out, b_in, b_out):
    def mod_group(g, half):
        return _slot(w_mod[g // 12], 512 * half, 256 * (g % 12), 4, 256)

    w = []
    for i in range(PAIRS):
        for col in (2 * E, 3 * E, 0, E):
            w += [_slot(a_in, 512 * half, col + 256 * i, 4, 256) for half in range(2)]
    for j in range(DPAIRS):
        w += [_slot(a_out, 512 * s, 256 * j, 4, 256) for s in range(4)]
    for c in range(4):
        w += [_slot(b_in, 256 * s, 2 * E + 512 * c, 2, 512) for s in range(4)]
    for i in range(PAIRS):
        for col in (E, 0):
            w += [_slot(b_in, 512 * half, col + 256 * i, 4, 256) for half in range(2)]
    for j in range(DPAIRS):
        w += [_slot(b_out, 512 * s, 256 * j, 4, 256) for s in range(4)]
    first = iter(np.concatenate([_slot(a_in, 256 * kp, col, 2, 256).reshape(P, 2, 256) for col in (2 * E, 3 * E)],
                                axis=2).reshape(P, SLOT) for kp in range(4))
    w[0:8] = [next(first), next(first), w[4], next(first), next(first), w[5], w[6], w[7]]

    def start_slot(kp, j):
        parts = [_slot(w_mod[0], 256 * j, col + 256 * kp, 2, 256).reshape(P, 2, 256) for col in (D, 0)]
        return np.concatenate(parts, axis=2).reshape(P, SLOT)

    def from_order(order, i, base):
        for n, what in enumerate(order):
            if not isinstance(what, str):
                yield w[base + what]
            elif what[0] == "s":
                yield start_slot(int(what[1]), order[:n].count(what))
            else:
                k = int(what[1])
                yield mod_group(8 + 2 * i + k // 2, k % 2)

    q = list(from_order(START_ORDER, 0, 0))
    for i in range(1, PAIRS):
        q += from_order(A_ORDER, i, 8 * i + LEAD)
    q += w[8 * PAIRS + LEAD:]
    return np.stack(q)


def kernel(x, c, norm_g, w_mod, b_mod, a_w_in, a_w_conv, a_w_out, b_w_in, b_ln_g, b_ln_b, b_w_s, b_b_s, b_w_out,
           final_g):
    import concourse.bacc as bacc
    from concourse.bass_utils import run_bass_kernel_spmd

    a = {k: np.asarray(v) for k, v in dict(x=x, c=c, norm_g=norm_g, w_mod=w_mod, b_mod=b_mod, a_w_in=a_w_in,
         a_w_conv=a_w_conv, a_w_out=a_w_out, b_w_in=b_w_in, b_ln_g=b_ln_g, b_ln_b=b_ln_b, b_w_s=b_w_s, b_b_s=b_b_s,
         b_w_out=b_w_out, final_g=final_g).items()}
    rows = [a["norm_g"], a["b_mod"], a["c"], a["b_ln_g"], a["b_ln_b"], a["final_g"], a["a_w_conv"][0].T]
    arrays = {
        "stream": _stream(a["w_mod"], a["a_w_in"][0], a["a_w_out"][0], a["b_w_in"][0], a["b_w_out"][0]),
        "xt": np.ascontiguousarray(a["x"][0].T.reshape(KD, P, S).transpose(1, 0, 2)),
        "cols": np.ascontiguousarray(np.concatenate([r.reshape(-1, P) for r in rows]).T),
        "wst": np.ascontiguousarray(a["b_w_s"][0].transpose(2, 0, 1).reshape(P, 8 * P)),
        "bs": np.ascontiguousarray(np.broadcast_to(a["b_b_s"][0].reshape(1, 8 * P), (P, 8 * P))),
    }
    nc = bacc.Bacc("TRN2", target_bir_lowering=False, num_devices=1)
    args = [nc.dram_tensor(f"in_{n}", v.shape, F32, kind="ExternalInput").ap() for n, v in arrays.items()]
    out = nc.dram_tensor("out_t", (P, KD, S), F32, kind="ExternalOutput").ap()
    build(nc, *args, out)
    r = run_bass_kernel_spmd(nc, [{f"in_{n}": v for n, v in arrays.items()}], core_ids=[0])
    return np.ascontiguousarray(r.results[0]["out_t"].transpose(2, 1, 0).reshape(1, S, D))
```
